# Optimizing a Trainium2 kernel written in Bass

```python
import math
import jax, jax.numpy as jnp
from jax import lax
import numpy as np

D_MODEL = 2048
BATCH = 1
SEQ = 256
DEPTH = 1

A_HEADS = 16
A_KV_HEADS = 4
A_HEAD_DIM = 64
A_GROUP = A_HEADS // A_KV_HEADS
WINDOW = 128
A_BLOCK = 128
A_Q_WIDTH = A_HEADS * A_HEAD_DIM
A_KV_WIDTH = A_KV_HEADS * A_HEAD_DIM
N_BUCKETS = 32
MAX_DISTANCE = 128
B_HEADS = 4
B_KEY_DIM = 128
B_VAL_DIM = 256
B_QK_WIDTH = B_HEADS * B_KEY_DIM
B_V_WIDTH = B_HEADS * B_VAL_DIM
B_GATE_RANK = 16
B_GATE_TAU = 16.0
B_CHUNK = 64
D_FF = -(-(8 * D_MODEL) // (3 * 256)) * 256
EPS = 1e-6
NEG_INF = -1e30

IN_SPLITS = (A_Q_WIDTH, A_KV_WIDTH, A_KV_WIDTH,
             B_QK_WIDTH, B_QK_WIDTH, B_V_WIDTH, B_GATE_RANK, B_V_WIDTH,
             D_MODEL, D_MODEL)
IN_WIDTH = sum(IN_SPLITS)


def rmsnorm(x, g):
    xf = x.astype(jnp.float32)
    y = xf * lax.rsqrt(jnp.mean(xf * xf, axis=-1, keepdims=True) + EPS)
    return (y * g.astype(jnp.float32)).astype(x.dtype)

def t5_causal_bucket(dist):
    max_exact = N_BUCKETS // 2
    d = jnp.maximum(dist, 0)
    large = max_exact + (jnp.log(jnp.maximum(d, 1).astype(jnp.float32) / max_exact)
                         / math.log(MAX_DISTANCE / max_exact)
                         * (N_BUCKETS - max_exact)).astype(jnp.int32)
    large = jnp.minimum(large, N_BUCKETS - 1)
    return jnp.where(d < max_exact, d, large)

def sliding_window_attention(q, k, v, sinks, rel_bias):
    B, S = q.shape[0], q.shape[1]
    nb = S // A_BLOCK
    qb = (q * (A_HEAD_DIM ** -0.5)).reshape(B, nb, A_BLOCK, A_KV_HEADS, A_GROUP, A_HEAD_DIM)
    pad = ((0, 0), (A_BLOCK, 0), (0, 0), (0, 0))
    kp = jnp.pad(k, pad).reshape(B, nb + 1, A_BLOCK, A_KV_HEADS, A_HEAD_DIM)
    vp = jnp.pad(v, pad).reshape(B, nb + 1, A_BLOCK, A_KV_HEADS, A_HEAD_DIM)
    kb = jnp.concatenate([kp[:, :-1], kp[:, 1:]], axis=2)
    vb = jnp.concatenate([vp[:, :-1], vp[:, 1:]], axis=2)
    s = jnp.einsum('bnqkgd,bnskd->bnkgqs', qb, kb).astype(jnp.float32)
    q_loc = jnp.arange(A_BLOCK)[:, None] + A_BLOCK
    k_loc = jnp.arange(2 * A_BLOCK)[None, :]
    dist = q_loc - k_loc
    band = (dist >= 0) & (dist < WINDOW)
    k_abs = jnp.arange(nb)[:, None, None] * A_BLOCK + k_loc[None] - A_BLOCK
    mask = band[None] & (k_abs >= 0)
    bias = rel_bias.astype(jnp.float32)[t5_causal_bucket(dist)]
    bias = bias.transpose(2, 0, 1).reshape(A_KV_HEADS, A_GROUP, A_BLOCK, 2 * A_BLOCK)
    s = jnp.where(mask[None, :, None, None], s + bias[None, None], NEG_INF)
    sink = sinks.astype(jnp.float32).reshape(A_KV_HEADS, A_GROUP)[None, None, :, :, None, None]
    m = jnp.maximum(jnp.max(s, axis=-1, keepdims=True), sink)
    p = jnp.exp(s - m)
    denom = jnp.sum(p, axis=-1, keepdims=True) + jnp.exp(sink - m)
    o = jnp.einsum('bnkgqs,bnskd->bnqkgd', (p / denom).astype(v.dtype), vb)
    return o.reshape(B, S, A_Q_WIDTH)

def gated_linear_attention(q, k, v, log_a):
    B, S = q.shape[0], q.shape[1]
    nc = S // B_CHUNK

    def chunks(t):
        return t.astype(jnp.float32).reshape(B, nc, B_CHUNK, B_HEADS, -1).transpose(0, 3, 1, 2, 4)

    qc = chunks(q) * (B_KEY_DIM ** -0.5)
    kc, vc, gc = chunks(k), chunks(v), chunks(log_a)
    b = jnp.cumsum(gc, axis=3)
    b_last = b[:, :, :, -1:, :]
    q_dec = qc * jnp.exp(b)
    k_dec = kc * jnp.exp(-b)
    k_state = kc * jnp.exp(b_last - b)
    causal = jnp.tril(jnp.ones((B_CHUNK, B_CHUNK), dtype=bool))
    att = jnp.where(causal, jnp.einsum('bhncd,bhnsd->bhncs', q_dec, k_dec), 0.0)
    o_intra = jnp.einsum('bhncs,bhnsv->bhncv', att, vc)
    dS = jnp.einsum('bhncd,bhncv->bhndv', k_state, vc)
    decay = jnp.exp(b_last[:, :, :, 0, :])

    def step(state, inp):
        dS_n, decay_n = inp
        return decay_n[..., None] * state + dS_n, state

    s0 = jnp.zeros((B, B_HEADS, B_KEY_DIM, B_VAL_DIM), jnp.float32)
    _, s_prev = lax.scan(step, s0, (dS.transpose(2, 0, 1, 3, 4), decay.transpose(2, 0, 1, 3)))
    s_prev = s_prev.transpose(1, 2, 0, 3, 4)
    o_inter = jnp.einsum('bhncd,bhndv->bhncv', q_dec, s_prev)
    o = o_intra + o_inter
    return o.transpose(0, 2, 3, 1, 4).reshape(B, S, B_HEADS, B_VAL_DIM)

def first_inputs(seed: int = 0) -> dict:
    key = jax.random.key(seed)
    ks = jax.random.split(key, 20)
    L = DEPTH

    def w(k, shape, fan_in):
        return jax.random.normal(k, shape, jnp.float32) * (fan_in ** -0.5)

    def gain(k, shape):
        return 1.0 + 0.02 * jax.random.normal(k, shape, jnp.float32)

    return {
        "x": jax.random.normal(ks[0], (BATCH, SEQ, D_MODEL), jnp.float32),
        "norm_mix_g": gain(ks[1], (L, D_MODEL)),
        "w_in": w(ks[2], (L, D_MODEL, IN_WIDTH), D_MODEL),
        "sinks": 0.5 * jax.random.normal(ks[3], (L, A_HEADS), jnp.float32),
        "rel_bias": 0.5 * jax.random.normal(ks[4], (N_BUCKETS, A_HEADS), jnp.float32),
        "w_gate_up": w(ks[5], (L, B_GATE_RANK, B_QK_WIDTH), B_GATE_RANK),
        "b_gate": 0.1 * jax.random.normal(ks[6], (L, B_QK_WIDTH), jnp.float32),
        "gla_norm_g": gain(ks[7], (L, B_VAL_DIM)),
        "w_proj_a": w(ks[8], (L, A_Q_WIDTH, D_MODEL), A_Q_WIDTH),
        "w_proj_b": w(ks[9], (L, B_V_WIDTH, D_MODEL), B_V_WIDTH),
        "w_out": w(ks[10], (L, D_MODEL, D_MODEL), D_MODEL),
        "norm_ffn_g": gain(ks[11], (L, D_MODEL)),
        "w_ffn_gate": w(ks[12], (L, D_MODEL, D_FF), D_MODEL),
        "w_ffn_up": w(ks[13], (L, D_MODEL, D_FF), D_MODEL),
        "w_ffn_down": w(ks[14], (L, D_FF, D_MODEL), D_FF),
        "norm_final_g": gain(ks[15], (D_MODEL,)),
    }

def first_block(x, norm_mix_g, w_in, sinks, rel_bias, w_gate_up, b_gate, gla_norm_g,
              w_proj_a, w_proj_b, w_out, norm_ffn_g, w_ffn_gate, w_ffn_up, w_ffn_down,
              norm_final_g):
    B, S = x.shape[0], x.shape[1]
    split_idx = [int(i) for i in np.cumsum(IN_SPLITS)[:-1]]
    h = x
    for l in range(DEPTH):
        u = rmsnorm(h, norm_mix_g[l])
        proj = u @ w_in[l]
        qa, ka, va, qb, kb, vb, g_low, ob_gate, gate_a, gate_b = jnp.split(proj, split_idx, axis=-1)
        ya = sliding_window_attention(
            qa.reshape(B, S, A_HEADS, A_HEAD_DIM),
            ka.reshape(B, S, A_KV_HEADS, A_HEAD_DIM),
            va.reshape(B, S, A_KV_HEADS, A_HEAD_DIM),
            sinks[l], rel_bias)
        ya = ya @ w_proj_a[l]
        log_a = jax.nn.log_sigmoid((g_low @ w_gate_up[l] + b_gate[l]).astype(jnp.float32)) / B_GATE_TAU
        ob = gated_linear_attention(
            qb.reshape(B, S, B_HEADS, B_KEY_DIM),
            kb.reshape(B, S, B_HEADS, B_KEY_DIM),
            vb.reshape(B, S, B_HEADS, B_VAL_DIM),
            log_a.reshape(B, S, B_HEADS, B_KEY_DIM))
        ob = rmsnorm(ob, gla_norm_g[l]).reshape(B, S, B_V_WIDTH).astype(x.dtype)
        yb = (ob * jax.nn.silu(ob_gate)) @ w_proj_b[l]
        merged = jax.nn.sigmoid(gate_a) * ya + jax.nn.sigmoid(gate_b) * yb
        h = h + (merged @ w_out[l]).astype(h.dtype)
        z = rmsnorm(h, norm_ffn_g[l])
        ff = (jax.nn.silu(z @ w_ffn_gate[l]) * (z @ w_ffn_up[l])) @ w_ffn_down[l]
        h = h + ff.astype(h.dtype)
    return rmsnorm(h, norm_final_g)


CHUNK = 64
Q_BLOCK = 128

CONV_WIDTH = 1024
CONV_K = 3

MLA_HEADS = 16
Q_LORA = 512
KV_LORA = 512
QK_NOPE = 128
QK_ROPE = 64
V_HEAD = 128
MLA_WIDTH = MLA_HEADS * V_HEAD
ROPE_THETA = 10000.0

MEM_TOKENS = 256
MEM_HEADS = 4
MEM_HEAD_DIM = 256
MEM_WIDTH = MEM_HEADS * MEM_HEAD_DIM

IN_SPLITS_2 = (
    CONV_WIDTH, CONV_WIDTH, CONV_WIDTH, CONV_WIDTH,
    Q_LORA, KV_LORA, QK_ROPE, MLA_WIDTH,
    MEM_WIDTH, MEM_WIDTH,
    D_MODEL, D_MODEL, D_MODEL,
)
IN_WIDTH_2 = sum(IN_SPLITS_2)


def rms_norm(x, g):
    xf = x.astype(jnp.float32)
    y = xf * lax.rsqrt(jnp.mean(xf * xf, axis=-1, keepdims=True) + EPS)
    return (y * g.astype(jnp.float32)).astype(x.dtype)

def apply_rope(x, cos, sin):
    x1, x2 = jnp.split(x.astype(jnp.float32), 2, axis=-1)
    return jnp.concatenate([x1 * cos - x2 * sin, x2 * cos + x1 * sin], axis=-1).astype(x.dtype)

def causal_depthwise_conv(u, w):
    k, c = w.shape
    return lax.conv_general_dilated(
        u, w[:, None, :].astype(u.dtype), window_strides=(1,), padding=[(k - 1, 0)],
        dimension_numbers=("NWC", "WIO", "NWC"), feature_group_count=c)

def mla_attention(c_q, c_kv, k_rope_raw, cos, sin, q_norm_g, w_uq, kv_norm_g, w_ukv,
                  qn_nope_g, qn_rope_g, kn_nope_g, kn_rope_g):
    b, s, _ = c_q.shape
    q = (rms_norm(c_q, q_norm_g) @ w_uq).reshape(b, s, MLA_HEADS, QK_NOPE + QK_ROPE)
    q_nope = rms_norm(q[..., :QK_NOPE], qn_nope_g)
    q_rope = apply_rope(rms_norm(q[..., QK_NOPE:], qn_rope_g), cos[:, :, None], sin[:, :, None])
    kv = (rms_norm(c_kv, kv_norm_g) @ w_ukv).reshape(b, s, MLA_HEADS, QK_NOPE + V_HEAD)
    k_nope = rms_norm(kv[..., :QK_NOPE], kn_nope_g)
    v = kv[..., QK_NOPE:]
    k_rope = apply_rope(rms_norm(k_rope_raw, kn_rope_g), cos, sin)
    scale = (QK_NOPE + QK_ROPE) ** -0.5
    n_blk = s // Q_BLOCK
    qn_blocks = q_nope.reshape(b, n_blk, Q_BLOCK, MLA_HEADS, QK_NOPE).transpose(1, 0, 2, 3, 4)
    qr_blocks = q_rope.reshape(b, n_blk, Q_BLOCK, MLA_HEADS, QK_ROPE).transpose(1, 0, 2, 3, 4)
    k_chunk = jnp.arange(s) // CHUNK

    def attend(args):
        qn, qr, blk = args
        sc = (jnp.einsum("bqhd,bkhd->bhqk", qn, k_nope, preferred_element_type=jnp.float32)
              + jnp.einsum("bqhr,bkr->bhqk", qr, k_rope, preferred_element_type=jnp.float32))
        q_chunk = (blk * Q_BLOCK + jnp.arange(Q_BLOCK)) // CHUNK
        allowed = k_chunk[None, :] <= q_chunk[:, None]
        p = jax.nn.softmax(jnp.where(allowed, sc * scale, -jnp.inf), axis=-1)
        return jnp.einsum("bhqk,bkhd->bqhd", p.astype(v.dtype), v)

    o = lax.map(attend, (qn_blocks, qr_blocks, jnp.arange(n_blk)))
    return o.transpose(1, 0, 2, 3, 4).reshape(b, s, MLA_WIDTH)

def memory_attention(q_raw, mem, mem_norm_g, w_mem_kv, qn_g, kn_g):
    b, s, _ = q_raw.shape
    m = mem.shape[1]
    q = rms_norm(q_raw.reshape(b, s, MEM_HEADS, MEM_HEAD_DIM), qn_g)
    k, v = jnp.split(rms_norm(mem, mem_norm_g) @ w_mem_kv, 2, axis=-1)
    k = rms_norm(k.reshape(b, m, MEM_HEADS, MEM_HEAD_DIM), kn_g)
    v = v.reshape(b, m, MEM_HEADS, MEM_HEAD_DIM)
    sc = jnp.einsum("bqhd,bmhd->bhqm", q, k, preferred_element_type=jnp.float32) * (MEM_HEAD_DIM ** -0.5)
    p = jax.nn.softmax(sc, axis=-1)
    return jnp.einsum("bhqm,bmhd->bqhd", p.astype(v.dtype), v).reshape(b, s, MEM_WIDTH)

def second_inputs(seed: int = 0) -> dict:
    key = jax.random.key(seed)
    ks = jax.random.split(key, 24)
    f32 = jnp.float32

    def w(k, shape, fan_in):
        return jax.random.normal(k, shape, f32) * (fan_in ** -0.5)

    def gain(k, shape):
        return 1.0 + 0.02 * jax.random.normal(k, shape, f32)

    x = jax.random.normal(ks[0], (BATCH, SEQ, D_MODEL), f32)
    offsets = jax.random.randint(ks[1], (BATCH, 1), 0, 64, dtype=jnp.int32) * CHUNK
    positions = (offsets + jnp.arange(SEQ, dtype=jnp.int32)[None, :]).astype(jnp.int32)
    mem = jax.random.normal(ks[2], (BATCH, MEM_TOKENS, D_MODEL), f32)
    L = DEPTH
    return {
        "x": x,
        "positions": positions,
        "mem": mem,
        "norm_g": gain(ks[3], (L, D_MODEL)),
        "w_in": w(ks[4], (L, D_MODEL, IN_WIDTH_2), D_MODEL),
        "conv_w": w(ks[5], (L, CONV_K, CONV_WIDTH), CONV_K),
        "w_conv_out": w(ks[6], (L, CONV_WIDTH, D_MODEL), CONV_WIDTH),
        "mla_q_norm_g": gain(ks[7], (L, Q_LORA)),
        "w_uq": w(ks[8], (L, Q_LORA, MLA_HEADS * (QK_NOPE + QK_ROPE)), Q_LORA),
        "mla_kv_norm_g": gain(ks[9], (L, KV_LORA)),
        "w_ukv": w(ks[10], (L, KV_LORA, MLA_HEADS * (QK_NOPE + V_HEAD)), KV_LORA),
        "mla_qn_nope_g": gain(ks[11], (L, QK_NOPE)),
        "mla_qn_rope_g": gain(ks[12], (L, QK_ROPE)),
        "mla_kn_nope_g": gain(ks[13], (L, QK_NOPE)),
        "mla_kn_rope_g": gain(ks[14], (L, QK_ROPE)),
        "w_mla_out": w(ks[15], (L, MLA_WIDTH, D_MODEL), MLA_WIDTH),
        "mem_norm_g": gain(ks[16], (L, D_MODEL)),
        "w_mem_kv": w(ks[17], (L, D_MODEL, 2 * MEM_WIDTH), D_MODEL),
        "mem_qn_g": gain(ks[18], (L, MEM_HEAD_DIM)),
        "mem_kn_g": gain(ks[19], (L, MEM_HEAD_DIM)),
        "w_mem_out": w(ks[20], (L, MEM_WIDTH, D_MODEL), MEM_WIDTH),
        "w_o": w(ks[21], (L, D_MODEL, D_MODEL), D_MODEL),
    }

def second_block(x, positions, mem, norm_g, w_in, conv_w, w_conv_out, mla_q_norm_g, w_uq,
              mla_kv_norm_g, w_ukv, mla_qn_nope_g, mla_qn_rope_g, mla_kn_nope_g, mla_kn_rope_g,
              w_mla_out, mem_norm_g, w_mem_kv, mem_qn_g, mem_kn_g, w_mem_out, w_o):
    half = QK_ROPE // 2
    inv_freq = jnp.power(ROPE_THETA, -jnp.arange(half, dtype=jnp.float32) / half)
    ang = positions.astype(jnp.float32)[..., None] * inv_freq
    cos, sin = jnp.cos(ang), jnp.sin(ang)
    split_at = np.cumsum(IN_SPLITS_2)[:-1].tolist()

    for l in range(DEPTH):
        h = rms_norm(x, norm_g[l])
        proj = h @ w_in[l]
        (c_gate, b_gate, u, conv_z, c_q, c_kv, k_rope_raw, mla_z,
         mem_q, mem_z, g_conv, g_mla, g_mem) = jnp.split(proj, split_at, axis=-1)

        conv_y = b_gate * causal_depthwise_conv(c_gate * u, conv_w[l])
        o_conv = (conv_y * jax.nn.silu(conv_z)) @ w_conv_out[l]

        mla_y = mla_attention(c_q, c_kv, k_rope_raw, cos, sin, mla_q_norm_g[l], w_uq[l],
                              mla_kv_norm_g[l], w_ukv[l], mla_qn_nope_g[l], mla_qn_rope_g[l],
                              mla_kn_nope_g[l], mla_kn_rope_g[l])
        o_mla = (mla_y * jax.nn.silu(mla_z)) @ w_mla_out[l]

        mem_y = memory_attention(mem_q, mem, mem_norm_g[l], w_mem_kv[l], mem_qn_g[l], mem_kn_g[l])
        o_mem = (mem_y * jax.nn.silu(mem_z)) @ w_mem_out[l]

        merged = (jax.nn.sigmoid(g_conv) * o_conv + jax.nn.sigmoid(g_mla) * o_mla
                  + jax.nn.sigmoid(g_mem) * o_mem)
        x = x + merged @ w_o[l]
    return x


def setup_inputs(seed=0):
    out = dict(first_inputs(seed))
    for name, value in second_inputs(seed + 1).items():
        if name != "x":
            out[name + "_2"] = value
    return out


def reference(
    x, norm_mix_g, w_in, sinks, rel_bias, w_gate_up, b_gate, gla_norm_g, w_proj_a, w_proj_b,
    w_out, norm_ffn_g, w_ffn_gate, w_ffn_up, w_ffn_down, norm_final_g, positions_2, mem_2,
    norm_g_2, w_in_2, conv_w_2, w_conv_out_2, mla_q_norm_g_2, w_uq_2, mla_kv_norm_g_2, w_ukv_2,
    mla_qn_nope_g_2, mla_qn_rope_g_2, mla_kn_nope_g_2, mla_kn_rope_g_2, w_mla_out_2,
    mem_norm_g_2, w_mem_kv_2, mem_qn_g_2, mem_kn_g_2, w_mem_out_2, w_o_2,
):
    x = first_block(
        x, norm_mix_g, w_in, sinks, rel_bias, w_gate_up, b_gate, gla_norm_g, w_proj_a, w_proj_b,
        w_out, norm_ffn_g, w_ffn_gate, w_ffn_up, w_ffn_down, norm_final_g,
    )
    return second_block(
        x, positions_2, mem_2, norm_g_2, w_in_2, conv_w_2, w_conv_out_2, mla_q_norm_g_2, w_uq_2,
        mla_kv_norm_g_2, w_ukv_2, mla_qn_nope_g_2, mla_qn_rope_g_2, mla_kn_nope_g_2,
        mla_kn_rope_g_2, w_mla_out_2, mem_norm_g_2, w_mem_kv_2, mem_qn_g_2, mem_kn_g_2,
        w_mem_out_2, w_o_2,
    )


_drawn_inputs = setup_inputs


def setup_inputs(seed=0):
    import zlib

    import numpy as np

    out = dict(_drawn_inputs(seed))
    spreads = {}
    factors = {'norm_mix_g': 3.198,
     'sinks': 20.586,
     'b_gate': 3.283,
     'gla_norm_g': 7.158,
     'norm_ffn_g': 3.615,
     'norm_g_2': 4.453,
     'mla_q_norm_g_2': 39.067,
     'mla_kv_norm_g_2': 45.684,
     'mla_qn_nope_g_2': 40.134,
     'mla_qn_rope_g_2': 56.894,
     'mla_kn_nope_g_2': 42.416,
     'mla_kn_rope_g_2': 60.505,
     'mem_norm_g_2': 36.856,
     'mem_qn_g_2': 38.818,
     'mem_kn_g_2': 44.351}
    for name, (base, spread) in spreads.items():
        noise = np.random.default_rng([zlib.crc32(name.encode()), seed]).standard_normal(out[name].shape)
        drawn = base * np.exp(spread * noise) if base else spread * noise
        out[name] = __import__('jax').numpy.asarray(drawn.astype(out[name].dtype))
    for name, factor in factors.items():
        out[name] = (out[name] * factor).astype(out[name].dtype)
    return out
```

```python
from contextlib import ExitStack, contextmanager

import numpy as np

import concourse.bass as bass
from concourse import mybir

ALU = mybir.AluOpType
ACT = mybir.ActivationFunctionType
AX = mybir.AxisListType
F32 = mybir.dt.float32
F32R = mybir.dt.float32r
I32 = mybir.dt.int32

P = 128
S = 256
T = S // P
D = 2048
KT = D // P
CW = 512
NEG = -1e30
EPS = 1e-6

AH, AKV, AD = 16, 4, 64
AG = AH // AKV
BH, BK, BV = 4, 128, 256
RANK = 16
TAU = 16.0
FF = 5632
FT = FF // P
NB = 32
C1 = {}
_o = 0
for _n, _w in (("qa", AH * AD), ("ka", AKV * AD), ("va", AKV * AD), ("qb", BH * BK), ("kb", BH * BK),
               ("vb", BH * BV), ("glow", RANK), ("ob", BH * BV), ("ga", D), ("gb", D)):
    C1[_n] = _o
    _o += _w
IN1 = _o
CONV, CONVK = 1024, 3
LORA = 512
MH, DN, DR, DV = 16, 128, 64, 128
EH, ED = 4, 256
C2 = {}
_o = 0
for _n, _w in (("cg", CONV), ("bg", CONV), ("u", CONV), ("cz", CONV), ("cq", LORA), ("ckv", LORA), ("kr", DR),
               ("mz", MH * DV), ("eq", EH * ED), ("ez", EH * ED), ("gc", D), ("gm", D), ("ge", D)):
    C2[_n] = _o
    _o += _w
IN2 = _o
ORDER = [0, 2, 1, 3]
MLA_SCALE = float(DN + DR) ** -0.5

GAINS = (("norm_mix_g", 16), ("norm_ffn_g", 16), ("norm_g_2", 16), ("mem_norm_g_2", 16), ("mla_q_norm_g_2", 4),
         ("mla_kv_norm_g_2", 4), ("conv_w_2", 24), ("mla_qn_nope_g_2", 1), ("mla_kn_nope_g_2", 1),
         ("mem_qn_g_2", 2), ("mem_kn_g_2", 2))
GCOL = {}
_o = 0
for _n, _w in GAINS:
    GCOL[_n] = _o
    _o += _w
NG = _o

GRAN = 1024
RAW, SPL = 8, 4
BIASW = 384


def shape_constants():
    i, j = np.arange(P)[:, None], np.arange(P)[None, :]
    same = (i // 64) == (j // 64)
    parts = {
        "ident": (i == j),
        "mla_mask": np.where((i < 64) & (j >= 64), NEG, 0.0),
        "tri": same & (i <= j),
        "after": same & (i > j),
        "causal": same & (i <= j),
        "in_chunk": (i // 64) == np.arange(2)[None, :],
        "inv_freq": np.broadcast_to(np.power(np.float32(10000.0), -np.arange(32, dtype=np.float32) / np.float32(32)), (P, 32)),
    }
    at, cols, o = {}, [], 0
    for name, a in parts.items():
        a = np.asarray(a, np.float32)
        at[name] = (o, a.shape[1])
        o += a.shape[1]
        cols.append(a)
    return at, np.ascontiguousarray(np.concatenate(cols, 1))


def bias_constants():
    dist = 255 - np.arange(BIASW)
    d = np.maximum(dist, 0)
    large = 16 + (np.log(np.maximum(d, 1).astype(np.float32) / np.float32(16)) / np.float32(np.log(8.0)) * np.float32(16)).astype(np.int32)
    bucket = np.where(d < 16, d, np.minimum(large, NB - 1))
    seen = (dist >= 0) & (dist < 128)
    onehot = ((np.arange(NB)[:, None] == bucket[None, :]) & seen[None, :]).astype(np.float32)
    mask = np.broadcast_to(np.where(seen, 0.0, NEG).astype(np.float32), (AH, BIASW))
    return onehot, np.ascontiguousarray(mask)


CONST_AT, CONST = shape_constants()
ONEHOT, BIAS_MASK = bias_constants()


class Count:

    def __init__(self):
        self.n, self.i, self.stride = 0, None, 0

    def at(self, k=0):
        v = self.n + k
        return v if self.i is None else v + self.i * self.stride

    def next(self, by=1):
        self.n += by
        return self.at()

    def rounds(self, size, k=0):
        v = (self.n + k) // size
        return v if self.i is None else v + self.i * (self.stride // size)

    def slot(self, size, k=0):
        assert self.stride % size == 0
        return (self.n + k) % size


@contextmanager
def engine_loop(eng, n, counts):
    starts = {c: c.n for c in counts}
    with eng.Fori(0, n) as i:
        for c, by in counts.items():
            c.i, c.stride = i, by
        yield i
        for c, by in counts.items():
            assert c.n - starts[c] == by, (c.n - starts[c], by)
    for c, by in counts.items():
        c.i, c.stride, c.n = None, 0, starts[c] + n * by


def need(eng, sem, value):
    if isinstance(value, int) and value <= 0:
        return
    eng.wait_ge(sem, value)


class Chunk:

    def __init__(self, name, x, x0, kts, per, w, weight, col, step=0):
        self.name, self.x, self.x0, self.kts, self.per, self.w = name, x, x0, kts, per, w
        self.weight, self.col, self.step = weight, col, step
        self.grans = kts // per


def segments():
    def one(name, x, x0, kts, weight, col, w=CW, per=2):
        return (name, 1, [Chunk(name, x, x0, kts, per, w, weight, col)])

    def pairs(name, x, x0, kts, weight, col, n=D // CW):
        return (name, n // 2, [Chunk(name, x, x0, kts, 2, CW, weight, col + k * CW, 2 * CW) for k in range(2)])

    out = []
    out += [one("qa", "A", 0, KT, "w_in", C1["qa"]), one("qa", "A", 0, KT, "w_in", C1["qa"] + CW)]
    out += [one("kva", "A", 0, KT, "w_in", C1["ka"])]
    out += [one("qb", "A", 0, KT, "w_in", C1["qb"]), one("kb", "A", 0, KT, "w_in", C1["kb"])]
    out += [one("vb", "A", 0, KT, "w_in", C1["vb"] + k * CW) for k in range(2)]
    out += [one("glow", "A", 0, KT, "w_in", C1["glow"], w=RANK, per=16)]
    out += [one("ob", "A", 0, KT, "w_in", C1["ob"] + k * CW) for k in range(2)]
    for ks in ((0, 1, 2), (3,)):
        out += [one("gate_a", "A", 0, KT, "w_in", C1["ga"] + k * CW) for k in ks]
        out += [one("proj_a", "B", 0, 8, "w_proj_a", k * CW) for k in ks]
    out += [pairs("gate_b", "A", 0, KT, "w_in", C1["gb"]), *(one("proj_b", "B", 8, 8, "w_proj_b", k * CW) for k in range(4))]
    out += [pairs("w_out", "A", 0, KT, "w_out", 0)]
    out += [("ffn_up", FF // CW, [Chunk("ffn_gate", "B", 0, KT, 2, CW, "w_ffn_gate", 0, CW),
                                  Chunk("ffn_up", "B", 0, KT, 2, CW, "w_ffn_up", 0, CW)])]
    out += [("ffn_down", FT // 4, [Chunk("ffn_down", "A", 0, 4, 1, 0, "w_ffn_down", 0)])]
    out += [pairs("mem_k", "B", 0, KT, "w_mem_kv_2", 0, 2), pairs("mem_v", "B", 0, KT, "w_mem_kv_2", EH * ED, 2)]
    for h in range(2):
        out += [one("ez", "A", 0, KT, "w_in_2", C2["ez"] + h * CW), one("eq", "A", 0, KT, "w_in_2", C2["eq"] + h * CW)]
        out += [one("ge", "A", 0, KT, "w_in_2", C2["ge"] + k * CW) for k in (2 * h, 2 * h + 1)]
    out += [pairs("mem_out", "B", 8, 8, "w_mem_out_2", 0)]
    for h in range(2):
        for n in ("cg", "u", "bg", "cz"):
            out += [one(n, "A", 0, KT, "w_in_2", C2[n] + h * CW)]
    out += [one("cq", "A", 0, KT, "w_in_2", C2["cq"]), one("ckv", "A", 0, KT, "w_in_2", C2["ckv"])]
    out += [one("kr", "A", 0, KT, "w_in_2", C2["kr"], w=DR, per=16)]
    mla = []
    for k in range(4):
        mla += [Chunk("uq", "B", 8, 4, 2, 384, "w_uq_2", k * 384, 4 * 384), Chunk("ukv", "B", 12, 4, 2, CW, "w_ukv_2", k * CW, 4 * CW)]
        j = k // 2
        if k % 2 == 0:
            mla += [Chunk("mz", "A", 0, KT, 2, CW, "w_in_2", C2["mz"] + j * CW, 2 * CW)]
        else:
            mla += [Chunk("gc", "A", 0, KT, 2, CW, "w_in_2", C2["gc"] + j * CW, 2 * CW),
                    Chunk("conv_out", "B", 0, 8, 2, CW, "w_conv_out_2", j * CW, 2 * CW)]
    out += [("mla", 2, mla)]
    out += [one("gm", "A", 0, KT, "w_in_2", C2["gm"] + k * CW) for k in range(4)]
    out += [one("mla_out", "B", 0, KT, "w_mla_out_2", k * CW) for k in range(4)]
    out += [pairs("w_o", "A", 0, KT, "w_o_2", 0)]
    return out


GATED = {"ob": "silu", "gate_a": "sigmoid", "ge": "sigmoid", "mz": "silu", "gc": "sigmoid", "gm": "sigmoid"}
TIMES = ("proj_a",)
MEM_BACK = (2, 2, 2, 2, 2, 1, 1, 1)
MLA_BACK = ((3, 2, 2, 1), (4, 3, 3, 2))
SWA_BACK = [(3, 2, 1)] * (AKV * T - 1) + [(3, 1, 0)]


def build(nc, ap, out, scratch):
    SEG = segments()
    ALL = [(c, k) for _, n, cs in SEG for k in range(n) for c in cs]

    with ExitStack() as ctx:
        def sb(name, shape, dt=F32):
            return ctx.enter_context(nc.sbuf_tensor(name, shape, dt))

        def sem(name):
            return ctx.enter_context(nc.semaphore(name))

        raw = sb("raw", [P, RAW, GRAN])
        w_hi = sb("w_hi", [P, SPL, GRAN], F32R)
        w_lo = sb("w_lo", [P, SPL, GRAN], F32R)
        w_hi32 = w_hi[:].bitcast(F32)
        XH = {n: sb(f"x_hi_{n}", [P, KT, S], F32R) for n in "AB"}
        XL = {n: sb(f"x_lo_{n}", [P, KT, S], F32R) for n in "AB"}
        xres = sb("xres", [P, T, D])
        stage = sb("stage", [P, 4, CW])
        work = sb("work", [P, 2048])
        etmp = sb("etmp", [P, T, CW])
        arena = sb("arena", [P, 54 * 256])
        cst = sb("cst", [P, CONST.shape[1]])
        grow = stage[:, 3, 0:P]
        gcol = sb("gcol", [P, NG])
        rope_g = sb("rope_g", [P, 2, DR])
        cs = sb("cs", [P, T, 2, 32])
        sinks = sb("sinks_sb", [P, AH])
        posi = sb("posi", [P, T], I32)
        sm = sb("sm", [P, 128])

        def con(name):
            o, n = CONST_AT[name]
            return cst[:, o:o + n]

        ident = con("ident")

        def area(kb, nkb):
            return arena[:, int(kb * 256):int((kb + nkb) * 256)]

        bias_t = area(0, 16).rearrange("p (h k) -> p h k", h=AH)
        qaT = area(16, 8).rearrange("p (h s) -> p h s", h=8)
        kaT = area(24, 4).rearrange("p (h s) -> p h s", h=4)
        va = area(28, 2).rearrange("p (t n) -> p t n", t=T)
        qb = area(30, 4).rearrange("p (t n) -> p t n", t=T)
        kb = area(34, 4).rearrange("p (t n) -> p t n", t=T)
        vb = area(38, 8).rearrange("p (t n) -> p t n", t=T)
        ob = area(46, 8).rearrange("p (t n) -> p t n", t=T)
        loga = area(0, 4).rearrange("p (t n) -> p t n", t=T)
        qdT = area(4, 4).rearrange("p (h s) -> p h s", h=BH)
        kdT = area(8, 4).rearrange("p (h s) -> p h s", h=BH)
        state = area(12, 2).rearrange("p (b n) -> p b n", b=2)
        w_up17 = area(14, 2)
        gla_g = area(16, 1)
        att = area(17, 1).rearrange("p (t n) -> p t n", t=T)
        og = area(18, 2).rearrange("p (t n) -> p t n", t=T)
        dec = area(20, 0.0625)
        glT = area(21, 1)
        gtmp = work[:, 0:1024].rearrange("p (t n) -> p t n", t=T)
        bias_row = work[0:AH, 0:BIASW]
        onehot = work[0:NB, 512:512 + BIASW]
        rel_b = work[0:NB, 1024:1024 + AH]
        bmask = work[0:AH, 1536:1536 + BIASW]
        merged1 = area(22, 16).rearrange("p (k t n) -> p k t n", k=4, t=T)
        side1 = area(0, 16).rearrange("p (k t n) -> p k t n", k=4, t=T)
        ffT = area(0, 44).rearrange("p (k s) -> p k s", s=S)
        fin_g = area(16, 8)
        memx = area(0, 16).rearrange("p (t n) -> p t n", t=T)
        memkT = area(32, 8).rearrange("p (h k s) -> p h k s", h=EH, k=2)
        memv = area(40, 8).rearrange("p (t n) -> p t n", t=T)
        cgt = area(0, 4).rearrange("p (t n) -> p t n", t=T)
        bgt = area(4, 4).rearrange("p (t n) -> p t n", t=T)
        vT = arena[:, 8 * 256:8 * 256 + 4 * (S + 2)].rearrange("p (k s) -> p k s", k=4)
        cvT = work[:, 0:1024]
        merged2 = area(16, 16).rearrange("p (k t n) -> p k t n", k=4, t=T)
        silz = area(32, 16).rearrange("p (k t n) -> p k t n", k=4, t=T)
        side2 = area(48, 4).rearrange("p (t n) -> p t n", t=T)
        side3 = area(0, 16).rearrange("p (k t n) -> p k t n", k=4, t=T)
        kx_mla = area(14, 2)
        rot = work[:, 12 * DN:12 * DN + 256].rearrange("p (k h n) -> p k h n", k=4, h=2)
        squares = work[:, 0:12 * DN].rearrange("p (k n) -> p k n", k=12)
        qs = area(0, 3).rearrange("p (t n) -> p t n", t=T)
        qnT = area(3, 2).rearrange("p (h s) -> p h s", h=2)
        qrT = area(5, 1)
        knT = area(7, 2).rearrange("p (h s) -> p h s", h=2)
        kvv = area(9, 2).rearrange("p (t n) -> p t n", t=T)
        rop = area(11, 1.5).rearrange("p (b n) -> p b n", b=3)
        krT = area(13, 1)
        ezs = area(48, 4).rearrange("p (t n) -> p t n", t=T)
        eqT = area(52, 2).rearrange("p (k s) -> p k s", k=2)

        acc = [ctx.enter_context(nc.psum_tensor(f"acc{i}", [P, T, 512], F32)) for i in range(2)]
        bankt = ctx.enter_context(nc.psum_tensor("banks", [P, 4, 512], F32))

        landed = [sem(f"landed{i}") for i in range(RAW)]
        hi_done, lo_done = sem("hi_done"), sem("lo_done")
        w_used = sem("w_used")
        acc_free = sem("acc_free")
        unit_src, unit_done, unit_free = sem("unit_src"), sem("unit_done"), sem("unit_free")
        act_req, act_done = sem("act_req"), sem("act_done")
        step = sem("step")
        astep = sem("astep")
        x_in, c_in, g_in, small_in = sem("x_in"), sem("c_in"), sem("g_in"), sem("small_in")
        b_in, b_row, b_ready = sem("b_in"), sem("b_row"), sem("b_ready")
        gla_in, mem_in, fin_in = sem("gla_in"), sem("mem_in"), sem("fin_in")
        x_split = sem("x_split")
        stored = sem("stored")
        out_ready = sem("out_ready")

        block = ctx.enter_context(nc.Block())

        def weight_src(c, g, i):
            w = ap[c.weight]
            col = c.col if c.step == 0 else c.col + i * c.step
            v = w.rearrange("(k p) n -> p k n", p=P)[:, g * c.per:(g + 1) * c.per, :]
            return v[:, :, bass.ds(col, c.w)]

        @block.sync
        def _(sp):
            sp.dma_start(xres[:], ap["x"].rearrange("(t p) n -> p t n", p=P)).then_inc(x_in, 16)
            G = Count()
            for name, n, chunks in SEG:
                def granule(dst_size, src, shape):
                    need(sp, lo_done, G.at(1 - RAW))
                    s = G.slot(RAW)
                    dst = raw[:, s, 0:dst_size]
                    if shape > 1:
                        dst = dst.rearrange("p (k n) -> p k n", k=shape)
                    sp.dma_start(dst, src).then_inc(landed[s], 16)
                    G.n += 1

                def body(i):
                    for c in chunks:
                        if c.name == "ffn_down":
                            for k in range(8):
                                src = ap["w_ffn_down"].rearrange("(k p) n -> p k n", p=P)
                                src = src[:, bass.ds(i * 4 + k // 2, 1), (k % 2) * 1024:(k % 2 + 1) * 1024]
                                granule(GRAN, src.rearrange("p a n -> p (a n)"), 1)
                        else:
                            for g in range(c.grans):
                                granule(c.per * c.w, weight_src(c, g, i), c.per)

                if n <= 2:
                    for i in range(n):
                        body(i)
                else:
                    per = 8 if name == "ffn_down" else sum(c.grans for c in chunks)
                    with engine_loop(sp, n, {G: per}) as i:
                        body(i)
                if name == "kva":
                    sp.wait_ge(b_ready, 16)
                    shifted = bass.AP(scratch.tensor, P - 1, [[BIASW, P], [P * (BIASW + 1), AH], [1, 2 * P]])
                    sp.dma_start(bias_t, shifted).then_inc(b_ready, 16)
            for t in range(T):
                sp.wait_ge(out_ready, t + 1)
                sp.dma_start(out.rearrange("(t p) n -> p t n", p=P)[:, t, :], xres[:, t, :]).then_inc(stored, 16)
            sp.wait_ge(stored, 16 * T)

        @block.tensor
        def _(pe):
            G, C, U, XS = Count(), Count(), Count(), Count()
            mm = pe.matmul

            def granule(c, g, bank, banks_of=None):
                pe.wait_ge(lo_done, G.at(1))
                s = G.slot(SPL)
                per, w = c.per, c.w
                hi = w_hi[:, s, 0:per * w].rearrange("p (k n) -> p k n", k=per)
                lo = w_lo[:, s, 0:per * w].rearrange("p (k n) -> p k n", k=per)
                for k in range(per):
                    kt = g * per + k
                    for t in range(T):
                        xh = XH[c.x][:, c.x0 + kt, t * P:(t + 1) * P]
                        xl = XL[c.x][:, c.x0 + kt, t * P:(t + 1) * P]
                        o = acc[bank][:, t, 0:w]
                        mm(o, xh, hi[:, k, :], start=(kt == 0), stop=False)
                        mm(o, xh, lo[:, k, :], start=False, stop=False)
                        last = mm(o, xl, hi[:, k, :], start=False, stop=(kt == c.kts - 1))
                last.then_inc(w_used, 1)
                G.n += 1

            def chunk(c):
                need(pe, acc_free, C.at(-1))
                for g in range(c.grans):
                    granule(c, g, C.slot(2))
                C.n += 1

            def run(name):
                n, chunks = next((n, cc) for nm, n, cc in SEG if nm == name)
                if n <= 1:
                    for c in chunks:
                        chunk(c)
                else:
                    with engine_loop(pe, n, {G: sum(c.grans for c in chunks), C: len(chunks)}):
                        for c in chunks:
                            chunk(c)

            singles = iter([c for nm, n, cc in SEG if n == 1 for c in cc])

            def one(name):
                chunk(next(c for c in singles if c.name == name))

            def background(*chunks):
                for c in chunks:
                    if isinstance(c, str):
                        c = next(x for x in singles if x.name == c)
                    behind.extend((c, g) for g in range(c.grans))
            behind = []

            def back(k):
                for c, g in behind[0:k]:
                    if g == 0:
                        need(pe, acc_free, C.at(-1))
                    granule(c, g, C.slot(2))
                    if g == c.grans - 1:
                        C.next()
                del behind[0:k]

            def activations():
                XS.n += 1
                pe.wait_ge(x_split, XS.n)

            def unit(fill):
                pe.wait_ge(unit_src, U.at(1))
                need(pe, unit_free, U.at(-3))
                u = U.slot(4)
                last = fill(bankt[:, u, :], stage[:, u, :])
                last.then_inc(unit_done, 1)
                U.n += 1

            def tr(o, i):
                return pe.transpose(o, i, ident[0:i.shape[0], 0:i.shape[0]])

            def turn_pair(b, s):
                for k in range(2):
                    for t in range(T):
                        last = tr(b[:, (2 * k + t) * P:(2 * k + t + 1) * P], s[:, t * 256 + k * P:t * 256 + (k + 1) * P])
                return last

            def turn_four(b, s, n=4, w=P):
                for k in range(n):
                    last = tr(b[0:w, k * P:(k + 1) * P], s[:, k * w:(k + 1) * w])
                return last

            def product_and_turn(name):
                one(name)
                for _ in range(3):
                    one(name)
                    unit(turn_pair)
                    unit(turn_pair)
                unit(turn_pair)
                unit(turn_pair)
                activations()

            pe.wait_ge(c_in, 16)
            pe.wait_ge(g_in, 16 * len(GAINS))
            unit(lambda b, s: tr(b[:, 0:NG], grow[0:NG, :]))
            for _ in range(KT // 2):
                unit(turn_pair)
            activations()
            one("qa")
            pe.wait_ge(b_in, 16 * 3)
            unit(lambda b, s: mm(b[0:AH, 0:BIASW], rel_b, onehot, start=True, stop=True))
            for name in ("qa", "kva"):
                one(name)
                for _ in range(4):
                    unit(lambda b, s: turn_four(b, s, 2))
            background("qb", "kb", "vb", "vb", "glow", "ob", "ob")
            back(3)
            for _ in range(2):
                unit(turn_four)
            for g in range(AKV):
                for b in range(T):
                    nk = (b + 1) * P
                    for u in range(2):
                        def fill(bk, s, u=u, nk=nk, b=b, g=g):
                            for k in range(2):
                                h = AG * g + 2 * k + u
                                o = 64 * u
                                last = mm(bk[:, k * nk:(k + 1) * nk], qaT[o:o + 64, h // 2, b * P:(b + 1) * P],
                                          kaT[o:o + 64, g, 0:nk], start=True, stop=True)
                            return last
                        unit(fill)
                    back(SWA_BACK[g * T + b][0])
                    nblk = 4 * (b + 1)
                    for u in range(nblk // 4):
                        def fill(bk, s, u=u):
                            for k in range(4):
                                last = tr(bk[:, k * P:(k + 1) * P], work[:, (4 * u + k) * P:(4 * u + k + 1) * P])
                            return last
                        unit(fill)
                    back(SWA_BACK[g * T + b][1])

                    def fill(bk, s, b=b, g=g):
                        for h in range(4):
                            p0 = ORDER.index(h) * (b + 1)
                            for kb_ in range(b + 1):
                                last = mm(bk[:, h * AD:(h + 1) * AD], work[:, 1024 + (p0 + kb_) * P:1024 + (p0 + kb_ + 1) * P],
                                          va[:, kb_, g * AD:(g + 1) * AD], start=(kb_ == 0), stop=(kb_ == b))
                        return last
                    unit(fill)
                    back(SWA_BACK[g * T + b][2])
                unit(turn_pair)
            activations()
            def fill(bk, s):
                for t in range(T):
                    last = tr(bk[0:RANK, t * P:(t + 1) * P], s[:, t * RANK:(t + 1) * RANK])
                return last
            unit(fill)
            background("gate_a", "gate_a", "gate_a", "proj_a", "proj_a", "proj_a")
            back(2)
            pe.wait_ge(gla_in, 16 * 3)
            for t in range(T):
                unit(lambda bk, s, t=t: mm(bk, glT[0:RANK + 1, t * P:(t + 1) * P], w_up17[0:RANK + 1, :], start=True, stop=True))
            back(3)
            for t in range(T):
                unit(lambda bk, s, t=t: mm(bk, con("tri"), loga[:, t, :], start=True, stop=True))
                unit(lambda bk, s, t=t: mm(bk, con("after"), loga[:, t, :], start=True, stop=True))
                back(2)
                unit(lambda bk, s, t=t: turn_four(bk, qb[:, t, :]))
                unit(turn_four)
                back(1)

            def fill(bk, s):
                for h in range(BH):
                    for t in range(T):
                        o = h * 4 + 2 * t
                        last = mm(bk[:, o:o + 2], loga[:, t, h * BK:(h + 1) * BK], con("in_chunk"), start=True, stop=True)
                return last
            unit(fill)
            back(1)
            for h in range(BH):
                for t in range(T):
                    unit(lambda bk, s, t=t, h=h: mm(bk[:, 0:P], kdT[:, h, t * P:(t + 1) * P], qdT[:, h, t * P:(t + 1) * P],
                                                    start=True, stop=True))
                back(2)

                def add_state(n, h=h):
                    t, c = divmod(n, 2)
                    unit(lambda bk, s: mm(bk[:, 0:BV], kb[64 * c:64 * c + 64, t, h * BK:(h + 1) * BK],
                                          vb[64 * c:64 * c + 64, t, h * BV:(h + 1) * BV], start=True, stop=True))

                def read_out(t, h=h):
                    def fill(bk, s):
                        last = mm(bk[:, 0:BV], att[:, t, :], vb[:, t, h * BV:(h + 1) * BV], start=True, stop=(t == 0),
                                  skip_group_check=True)
                        for c in range(2):
                            n = 2 * t + c
                            if n:
                                last = mm(bk[64 * c:64 * c + 64, 0:BV], qdT[:, h, n * 64:(n + 1) * 64], state[:, n % 2, :],
                                          start=False, stop=True, skip_group_check=True)
                        return last
                    unit(fill)
                add_state(0)
                read_out(0)
                back(1)
                add_state(1)
                add_state(2)
                read_out(1)
                back(3)
                unit(turn_pair)
            activations()
            for nm in ("gate_a", "proj_a"):
                one(nm)
            run("gate_b")
            product_and_turn("proj_b")
            run("w_out")
            for _ in range(KT // 2):
                unit(turn_pair)
            activations()
            n, chunks = next((n, cc) for nm, n, cc in SEG if nm == "ffn_up")
            chunk(chunks[0])
            chunk(chunks[1])
            with engine_loop(pe, (n - 1) // 2, {G: 32, C: 4, U: 4}):
                for _ in range(2):
                    chunk(chunks[0])
                    for _ in range(2):
                        unit(turn_pair)
                    chunk(chunks[1])
            for _ in range(2):
                unit(turn_pair)
            need(pe, acc_free, C.at(0))
            need(pe, unit_free, U.at(0))
            DG = [acc[0][:, 0, :], acc[0][:, 1, :], acc[1][:, 0, :], acc[1][:, 1, :]] + [bankt[:, k, :] for k in range(4)]

            def down(first, last_pass):
                for k in range(4):
                    if k == 0:
                        XS.n += 1
                        pe.wait_ge(x_split, XS.at(0))
                    for half in range(2):
                        pe.wait_ge(lo_done, G.at(1))
                        s = G.slot(SPL)
                        for t in range(T):
                            xh = XH["A"][:, par4(k), t * P:(t + 1) * P]
                            xl = XL["A"][:, par4(k), t * P:(t + 1) * P]
                            for q in range(2):
                                o = DG[t * 4 + half * 2 + q]
                                a, z = w_hi[:, s, q * 512:(q + 1) * 512], w_lo[:, s, q * 512:(q + 1) * 512]
                                f = first and k == 0
                                e = last_pass and k == 3
                                mm(o, xh, a, start=f, stop=False, skip_group_check=True)
                                mm(o, xh, z, start=False, stop=False, skip_group_check=True)
                                last = mm(o, xl, a, start=False, stop=e, skip_group_check=True)
                        last.then_inc(w_used, 1)
                        G.n += 1

            par = [0]

            def par4(k):
                return par[0] * 4 + k
            down(True, False)
            par[0] = 1
            down(False, False)
            with engine_loop(pe, (FT // 4 - 3) // 2, {G: 16, XS: 2}):
                for q in range(2):
                    par[0] = q
                    down(False, False)
            par[0] = 0
            down(False, True)
            for _ in range(KT // 2):
                unit(turn_pair)
            activations()
            one("mem_k")
            one("mem_k")
            unit(turn_pair)
            unit(turn_pair)
            background("mem_v", "mem_v")
            back(3)
            unit(turn_pair)
            unit(turn_pair)
            for p in range(KT // 2):
                unit(turn_pair)
                back(MEM_BACK[p])
            activations()
            for h2 in range(2):
                one("ez")
                one("eq")
                background("ge", "ge")
                back(2)
                for hh in range(2):
                    h = 2 * h2 + hh
                    unit(turn_pair)
                    back(2)

                    def fill(bk, s, h=h):
                        for t in range(T):
                            for k in range(2):
                                last = mm(bk[:, t * 256:(t + 1) * 256], eqT[:, k, t * P:(t + 1) * P], memkT[:, h, k, :],
                                          start=(k == 0), stop=(k == 1))
                        return last
                    unit(fill)
                    back(2)

                    def fill(bk, s):
                        for k in range(4):
                            last = tr(bk[:, k * P:(k + 1) * P], work[:, k * P:(k + 1) * P])
                        return last
                    unit(fill)
                    back(1)

                    def fill(bk, s, h=h):
                        for t in range(T):
                            for k in range(2):
                                last = mm(bk[:, t * 256:(t + 1) * 256], work[:, 1024 + (2 * t + k) * P:1024 + (2 * t + k + 1) * P],
                                          memv[:, k, h * ED:(h + 1) * ED], start=(k == 0), stop=(k == 1))
                        return last
                    unit(fill)
                    back(1)
                    unit(turn_pair)
                    back(1)
            activations()
            run("mem_out")
            for h in range(2):
                one("cg")
                if h == 1:
                    unit(turn_pair)
                    unit(turn_pair)
                one("u")
                one("bg")
                unit(turn_pair)
                unit(turn_pair)
                one("cz")
            for name in ("cq", "ckv", "kr"):
                one(name)
                unit(turn_pair)
                unit(turn_pair)
            unit(lambda b, s: turn_four(b, s, 2))
            activations()
            n, chunks = next((n, cc) for nm, n, cc in SEG if nm == "mla")

            def mla_pair(ks, uq, ukv, *others):
                chunk(uq)
                chunk(ukv)
                background(*others)
                back(ks[0])

                def fill(bk, s):
                    for h in range(2):
                        for t in range(T):
                            last = tr(bk[:, (2 * h + t) * P:(2 * h + t + 1) * P], s[:, t * 256 + h * P:t * 256 + (h + 1) * P])
                    return last
                unit(fill)

                unit(lambda b, s: turn_four(b, s, 2))
                unit(turn_pair)
                back(ks[1])
                for h in range(2):
                    def fill(bk, s, h=h):
                        for t in range(T):
                            nk = (t + 1) * P
                            o = bk[:, t * P:t * P + nk]
                            mm(o, qnT[:, h, t * P:(t + 1) * P], knT[:, h, 0:nk], start=True, stop=False)
                            last = mm(o, qrT[h * DR:(h + 1) * DR, t * P:(t + 1) * P], krT[h * DR:(h + 1) * DR, 0:nk],
                                      start=False, stop=True)
                        return last
                    unit(fill)
                back(ks[2])
                for h in range(2):
                    def fill(bk, s, h=h):
                        for k in range(3):
                            last = tr(bk[:, k * P:(k + 1) * P], work[:, h * 384 + k * P:h * 384 + (k + 1) * P])
                        return last
                    unit(fill)
                back(ks[3])

                def fill(bk, s):
                    for h in range(2):
                        for t in range(T):
                            o = bk[:, t * 256 + h * DV:t * 256 + (h + 1) * DV]
                            for k in range(t + 1):
                                last = mm(o, work[:, 1024 + h * 384 + (t + k) * P:1024 + h * 384 + (t + k + 1) * P],
                                          kvv[:, k, h * DV:(h + 1) * DV], start=(k == 0), stop=(k == t))
                    return last
                unit(fill)
            with engine_loop(pe, n, {G: 56, C: 14, U: 32}):
                for k in range(2):
                    mla_pair(MLA_BACK[0], *chunks[7 * k:7 * k + 3])
                    mla_pair(MLA_BACK[1], *chunks[7 * k + 3:7 * k + 7])
            background("gm", "gm", "gm")
            for _ in range(KT // 2):
                unit(turn_pair)
                back(3)
            one("gm")
            activations()
            product_and_turn("mla_out")
            run("w_o")

        class Walk:

            def __init__(self, eng):
                self.eng = eng
                self.G, self.E, self.C, self.U, self.R = Count(), Count(), Count(), Count(), Count()
                self.next, self.part = 0, 0

            def split_next(self):
                if self.next:
                    self.ahead(self.head(self.next - 1, None) - self.part)
                if self.next < len(ALL):
                    self.next, self.part = self.next + 1, 0
                    self.ahead(self.head(self.next - 1, SPL))
                else:
                    self.next += 1

            def head(self, k, most):
                c = ALL[k][0]
                return 0 if c.name == "ffn_down" else len(range(c.grans)[:most])

            def ahead(self, n):
                for _ in range(n):
                    if self.part == self.head(self.next - 1, None):
                        self.next, self.part = self.next + 1, 0
                    c = ALL[self.next - 1][0]
                    self.split(c.per * c.w)
                    self.part += 1

            def more(self):
                self.ahead(min(2, self.head(self.next - 1, None) - self.part))

            def background(self, n, begun=True, lead=0):
                first = self.next - 1 if begun else self.next
                self.lead = self.part if begun else 0
                self.ahead(lead)
                self.lead += lead
                self.behind = [ALL[first + k][0] for k in range(n)]
                self.most = 1000 if begun else sum(c.grans for c in self.behind) - lead
                self.left, self.after = self.behind[0].grans, first + n + 1
                self.finished = []

            def back(self, k):
                n = min(SPL - self.lead, self.most)
                if len(self.finished) > 1 or (self.finished and self.behind and self.behind[0].grans < SPL):
                    while self.finished:
                        self.take(self.finished.pop(0))
                self.ahead(n)
                while self.finished:
                    self.take(self.finished.pop(0))
                self.most -= n
                self.lead += n - k
                assert self.lead >= 0
                for _ in range(k):
                    self.left -= 1
                    if self.left == 0:
                        self.finished.append(self.behind.pop(0))
                        self.left = self.behind[0].grans if self.behind else 0

            def back_end(self):
                assert not self.behind
                while self.finished:
                    self.take(self.finished.pop(0))
                if self.most:
                    while (self.next, self.part) != (self.after, self.head(self.after - 1, SPL)):
                        self.ahead(1)

            def bank(self, k=0):
                return bankt[:, self.U.slot(4, k), :]

            def slot(self, k=0):
                return stage[:, self.U.slot(4, k), :]

        @block.scalar
        def _(act):
            act.dma_start(cst[:], ap["const"]).then_inc(c_in, 16)
            o = 0
            for nm, rows in GAINS:
                act.dma_start(grow[o:o + rows, :], ap[nm].rearrange("(r p) -> r p", p=P)).then_inc(g_in, 16)
                o += rows
            act.dma_start(onehot, ap["onehot"]).then_inc(b_in, 16)
            act.dma_start(rel_b, ap["rel_bias"]).then_inc(b_in, 16)
            act.dma_start(bmask, ap["bias_mask"]).then_inc(b_in, 16)
            act.dma_start(sinks[:], ap["sinks"].rearrange("(a n) -> a n", a=1).to_broadcast([P, AH])).then_inc(small_in, 16)
            act.dma_start(rope_g[:, 0, :], ap["mla_qn_rope_g_2"].rearrange("(a n) -> a n", a=1).to_broadcast([P, DR])).then_inc(small_in, 16)
            act.dma_start(rope_g[:, 1, :], ap["mla_kn_rope_g_2"].rearrange("(a n) -> a n", a=1).to_broadcast([P, DR])).then_inc(small_in, 16)
            for t in range(T):
                act.dma_start(posi[:, t:t + 1], ap["positions_2"].rearrange("(t p a) -> t p a", p=P, a=1)[t]).then_inc(small_in, 16)

            W = Walk(act)
            A = Count()

            def split(n):
                s, r = W.G.slot(SPL), W.G.slot(RAW)
                act.wait_ge(landed[r], (W.G.rounds(RAW) + 1) * 16)
                need(act, w_used, W.G.at(1 - SPL))
                act.activation(w_hi[:, s, 0:n], raw[:, r, 0:n], ACT.Copy).then_inc(hi_done, 1)
                W.G.n += 1
            W.split = split

            def rsqrt(ms, y):
                act.wait_ge(act_req, W.R.at(1))
                act.activation(y, ms, ACT.Ln).then_inc(astep, 1)
                act.wait_ge(astep, A.next())
                act.activation(y, y, ACT.Exp, scale=-0.5).then_inc(act_done, 1)
                W.R.next()

            def split_unit(dst, kt, gain=None):
                act.wait_ge(unit_done, W.U.at(1))
                b = W.bank()
                act.wait_ge(act_req, W.R.at(1))
                if gain is None:
                    ins = act.activation(XH[dst][:, kt:kt + 2, :].rearrange("p k s -> p (k s)"), b, ACT.Copy)
                else:
                    for k in range(2):
                        ins = act.activation(XH[dst][:, kt + k, :], b[:, k * S:(k + 1) * S], ACT.Copy,
                                             scale=gcol[:, gain + k:gain + k + 1])
                ins.then_inc(act_done, 1)
                W.R.next()
                W.U.n += 1

            def norm_split(dst, kt0, kts, gain, back=(), with_rsqrt=True):
                if gain is not None and with_rsqrt:
                    rsqrt(sm[:, 0:2], sm[:, 2:4])
                for p in range(kts // 2 + 2):
                    if back and p < kts // 2:
                        W.back(back[p])
                    if p >= 2:
                        split_unit(dst, kt0 + 2 * (p - 2), None if gain is None else gain + 2 * (p - 2))

            def product_and_turn(dst):
                plain()
                for k in range(4):
                    if k < 3:
                        plain()
                    split_unit(dst, 4 * k)
                    split_unit(dst, 4 * k + 2)

            def skip_units(n):
                W.U.n += n

            def evac_exp(w=CW):
                act.wait_ge(act_req, W.R.at(1))
                act.activation(etmp[:, :, 0:w], acc[W.C.slot(2)][:, :, 0:w], ACT.Exp, scale=-1.0).then_inc(act_done, 1)
                W.R.n += 1

            def done_chunk():
                W.C.n += 1

            def plain(n=1):
                for _ in range(n):
                    W.split_next()
                    done_chunk()

            def gated(n=1):
                for _ in range(n):
                    W.split_next()
                    evac_exp()
                    W.more()
                    done_chunk()

            def softmax(heads, width, off=0):
                for h in range(heads):
                    act.wait_ge(act_req, W.R.at(1))
                    w, o = width(h)
                    act.activation(work[:, o:o + w], work[:, o:o + w], ACT.Exp, bias=sm[:, 16 + h:17 + h],
                                          accum_out=sm[:, 24 + h:25 + h]).then_inc(act_done, 1)
                    W.R.next()

            def take(c):
                if c.name in GATED:
                    evac_exp()
                done_chunk()
            W.take = take

            skip_units(1)
            W.split_next()
            norm_split("A", 0, KT, GCOL["norm_mix_g"])
            act.wait_ge(act_req, W.R.at(1))
            act.activation(cs[:].rearrange("p t c n -> p (t c n)"), cs[:].rearrange("p t c n -> p (t c n)"), ACT.Sin).then_inc(act_done, 1)
            W.R.next()
            plain()
            act.wait_ge(b_row, 1)
            copies = scratch.rearrange("h (q j) -> h q j", j=BIASW + 1)[:, :, 0:BIASW]
            act.dma_start(copies, bias_row.unsqueeze(1).to_broadcast([AH, P, BIASW])).then_inc(b_ready, 16)
            skip_units(1)
            plain()
            skip_units(4)
            plain()
            skip_units(4)
            W.background(7)
            W.back(3)
            skip_units(2)
            for g in range(AKV):
                for b in range(T):
                    W.back(SWA_BACK[g * T + b][0])
                    skip_units(2)
                    nk = (b + 1) * P
                    softmax(4, lambda h, nk=nk: (nk, h * nk))
                    act.wait_ge(act_req, W.R.at(1))
                    act.activation(sm[:, 32:36], sm[:, 28:32], ACT.Exp).then_inc(act_done, 1)
                    W.R.next()
                    W.back(SWA_BACK[g * T + b][1])
                    skip_units(b + 1)
                    W.back(SWA_BACK[g * T + b][2])
                    skip_units(1)
                split_unit("B", 2 * g)
            W.back_end()
            act.wait_ge(act_req, W.R.at(1))
            act.dma_start(w_up17[0:RANK, :], ap["w_gate_up"]).then_inc(gla_in, 16)
            act.dma_start(w_up17[RANK:RANK + 1, :], ap["b_gate"].rearrange("(a n) -> a n", a=1)).then_inc(gla_in, 16)
            act.dma_start(gla_g, ap["gla_norm_g"].rearrange("(a n) -> a n", a=1).to_broadcast([P, BV])).then_inc(gla_in, 16)
            act.sem_inc(act_done, 1)
            W.R.next()
            W.background(6)
            W.back(2)
            skip_units(1)
            W.back(3)
            for t in range(T):
                act.wait_ge(act_req, W.R.at(1))
                act.activation(gtmp[:, t, :], gtmp[:, t, :], ACT.Exp, scale=-1.0).then_inc(astep, 1)
                act.wait_ge(astep, A.next())
                act.activation(gtmp[:, t, :], gtmp[:, t, :], ACT.Ln, bias=1.0).then_inc(act_done, 1)
                W.R.next()
                skip_units(1)
            for t in range(T):
                W.back(2)
                act.wait_ge(unit_done, W.U.at(1))
                act.wait_ge(act_req, W.R.at(1))
                act.activation(gtmp[:, 0, :], W.bank(), ACT.Exp)
                act.activation(gtmp[:, 1, :], W.bank(), ACT.Exp, scale=-1.0).then_inc(act_done, 1)
                W.R.next()
                skip_units(1)
                act.wait_ge(unit_done, W.U.at(1))
                act.wait_ge(act_req, W.R.at(1))
                act.activation(gtmp[:, 0, :], W.bank(), ACT.Exp).then_inc(act_done, 1)
                W.R.next()
                skip_units(1)
                W.back(1)
                skip_units(2)
            W.back(1)
            act.wait_ge(unit_done, W.U.at(1))
            act.wait_ge(act_req, W.R.at(1))
            act.activation(dec[:, 0:16], W.bank()[:, 0:16], ACT.Exp).then_inc(act_done, 1)
            W.R.next()
            skip_units(1)
            for h in range(BH):
                W.back(2)
                W.back(1)
                W.back(3)
                skip_units(7)
                rsqrt(sm[:, 0:2], sm[:, 2:4])
                split_unit("B", 8 + 2 * h)
            W.back_end()
            gated()
            plain()
            gated(4)
            product_and_turn("A")
            plain(4)
            norm_split("B", 0, KT, GCOL["norm_ffn_g"])

            def ffn_pass(units=2):
                gated()
                skip_units(units)
                plain()
            n = FF // CW
            ffn_pass(0)
            with engine_loop(act, (n - 3) // 2, {W.G: 32, W.C: 4, W.R: 2, W.U: 4}):
                ffn_pass()
                ffn_pass()
            W.next += 2 * (n - 5)
            ffn_pass()
            ffn_pass()
            skip_units(2)

            def down_pass(q, i, last=False):
                act.wait_ge(act_req, W.R.at(1))
                if last:
                    act.dma_start(memx, ap["mem_2"].rearrange("(t p) n -> p t n", p=P)).then_inc(mem_in, 16)
                    act.dma_start(fin_g, ap["norm_final_g"].rearrange("(a n) -> a n", a=1).to_broadcast([P, D])).then_inc(fin_in, 16)
                for k in range(4):
                    ins = act.activation(XH["A"][:, 4 * q + k, :], ffT[:, bass.ds(i + k, 1), :].rearrange("p a s -> p (a s)"), ACT.Copy)
                ins.then_inc(act_done, 1)
                W.R.next()
                for _ in range(8):
                    split(GRAN)
            down_pass(0, 0)
            down_pass(1, 4)
            with engine_loop(act, (FT // 4 - 3) // 2, {W.G: 16, W.R: 2}) as i:
                down_pass(0, i * 8 + 8)
                down_pass(1, i * 8 + 12)
            down_pass(0, FT - 4, True)
            W.next += FT // 4 - 1
            rsqrt(sm[:, 0:2], sm[:, 2:4])
            W.split_next()
            norm_split("B", 0, KT, GCOL["mem_norm_g_2"], (), False)
            W.split_next()
            rsqrt(sm[:, 0:2], sm[:, 2:4])
            done_chunk()
            W.split_next()
            rsqrt(sm[:, 0:4], sm[:, 4:8])
            rsqrt(sm[:, 0:2], sm[:, 2:4])
            skip_units(2)
            rsqrt(sm[:, 0:4], sm[:, 4:8])
            done_chunk()
            W.background(2)
            W.back(3)
            skip_units(2)
            norm_split("A", 0, KT, GCOL["norm_g_2"], MEM_BACK, False)
            W.back_end()
            for h2 in range(2):
                gated()
                W.split_next()
                done_chunk()
                W.background(2)
                W.back(2)
                rsqrt(sm[:, 0:4], sm[:, 4:8])
                for hh in range(2):
                    W.back(2)
                    W.back(2)
                    softmax(2, lambda t: (256, t * 256))
                    W.back(1)
                    W.back(1)
                    W.back(1)
                    skip_units(4)
                    split_unit("B", 8 + 4 * h2 + 2 * hh)
                W.back_end()
            plain(4)
            def conv_split(h):
                for p in range(2):
                    act.wait_ge(act_req, W.R.at(1))
                    kt = 4 * h + 2 * p
                    act.activation(XH["B"][:, kt:kt + 2, :].rearrange("p k s -> p (k s)"), cvT[:, p * 512:(p + 1) * 512],
                                   ACT.Copy).then_inc(act_done, 1)
                    W.R.next()
                    skip_units(1)
            for h in range(2):
                plain()
                if h == 1:
                    conv_split(0)
                plain(2)
                skip_units(2)
                gated()
            plain()
            conv_split(1)
            rsqrt(sm[:, 0:2], sm[:, 2:4])
            plain()
            for p in range(2):
                split_unit("B", 8 + 2 * p, GCOL["mla_q_norm_g_2"] + 2 * p)
            rsqrt(sm[:, 0:2], sm[:, 2:4])
            done_chunk()
            for p in range(2):
                split_unit("B", 12 + 2 * p, GCOL["mla_kv_norm_g_2"] + 2 * p)
            rsqrt(sm[:, 0:2], sm[:, 2:4])
            skip_units(1)

            def mla_pair(pr):
                if pr == 0:
                    W.ahead(4)
                done_chunk()
                W.background(1 + pr % 2, False, 2)
                done_chunk()
                ks = MLA_BACK[pr % 2]
                W.back(ks[0])
                rsqrt(sm[:, 0:12], sm[:, 12:24])
                W.back(ks[1])
                skip_units(3)
                W.back(ks[2])
                skip_units(2)
                softmax(4, lambda k: (P if k % 2 == 0 else 2 * P, (k // 2) * 384 + (k % 2) * P))
                W.back(ks[3])
                skip_units(2)
                if pr < 3:
                    W.ahead(4)
                W.back_end()
                skip_units(1)
            with engine_loop(act, 2, {W.G: 56, W.C: 14, W.U: 32, W.R: 24, A: 4}):
                for pr in range(4):
                    mla_pair(pr)
            W.next += 14
            W.split_next()
            W.background(3)
            norm_split("B", 0, KT, None, (3,) * (KT // 2))
            W.back_end()
            gated()
            product_and_turn("A")
            plain(4)

        @block.vector
        def _(dve):
            W = Walk(dve)
            V = Count()
            XS = Count()
            SRC, REQ = Count(), Count()

            def split(n):
                s, r = W.G.slot(SPL), W.G.slot(RAW)
                dve.wait_ge(hi_done, W.G.at(1))
                dve.tensor_tensor(w_lo[:, s, 0:n], raw[:, r, 0:n], w_hi32[:, s, 0:n], ALU.subtract).then_inc(lo_done, 1)
                W.G.n += 1
            W.split = split

            def tell(sem_):
                dve.sem_inc(sem_, 1)

            def this():
                return ALL[W.next - 2][0]

            TT, TS, STT, CP = dve.tensor_tensor, dve.tensor_scalar, dve.scalar_tensor_tensor, dve.tensor_copy

            def ttr(o, a, b, acc_):
                return dve.tensor_tensor_reduce(out=o, in0=a, in1=b, scale=1.0, scalar=0.0, op0=ALU.mult, op1=ALU.add,
                                                accum_out=acc_)

            def rsqrt(n, dim, a=None):
                ms, y, q = sm[:, 0:n], sm[:, n:2 * n], sm[:, 96:96 + n]
                if dim is not None:
                    TS(ms, ms, 1.0 / dim, EPS, ALU.mult, ALU.add).then_inc(act_req, 1)
                    dve.wait_ge(act_req, REQ.next())
                else:
                    dve.sem_inc(act_req, 1)
                    REQ.n += 1
                dve.wait_ge(act_done, W.R.next())
                TT(q, y, y, ALU.mult).then_inc(step, 1)
                dve.wait_ge(step, V.next())
                TT(q, q, ms, ALU.mult).then_inc(step, 1)
                dve.wait_ge(step, V.next())
                TS(q, q, -0.5, 1.5, ALU.mult, ALU.add).then_inc(step, 1)
                dve.wait_ge(step, V.next())
                TT(y, y, q, ALU.mult).then_inc(step, 1)
                dve.wait_ge(step, V.next())

            def row_rstd(x, w):
                nq = w // CW
                for t in range(T):
                    for q in range(nq):
                        v = x[:, t, q * CW:(q + 1) * CW]
                        ttr(etmp[:, q % 2, :], v, v, sm[:, 4 + t * nq + q:5 + t * nq + q]).then_inc(step, 1)
                        if q % 2 or nq == 1:
                            dve.wait_ge(step, V.at(1))
                        V.next()
                dve.tensor_reduce(sm[:, 0:2], sm[:, 4:4 + T * nq].rearrange("p (t q) -> p t q", t=T), AX.X, ALU.add).then_inc(step, 1)
                dve.wait_ge(step, V.next())
                rsqrt(2, w)

            def row_part(x, k):
                for t in range(T):
                    v = x[:, t, k * CW:(k + 1) * CW]
                    ins = ttr(etmp[:, t, :], v, v, sm[:, 4 + 4 * t + k:5 + 4 * t + k])
                ins.then_inc(step, 1)
                dve.wait_ge(step, V.next())

            def row_end():
                dve.tensor_reduce(sm[:, 0:2], sm[:, 4:12].rearrange("p (t q) -> p t q", t=T), AX.X, ALU.add).then_inc(step, 1)
                dve.wait_ge(step, V.next())
                rsqrt(2, D)

            def turn_and_split(dst, kt0, kts, gain, fill, back=()):
                n, lag = kts // 2, 2
                for p in range(n + lag):
                    if p < n:
                        fill(p, stage[:, W.U.slot(4, min(p, lag)), :].rearrange("p (t n) -> p t n", t=T))
                        if back:
                            W.back(back[p])
                        else:
                            ask_high()
                    if p >= lag:
                        low_part(dst, kt0 + 2 * (p - lag), None if gain is None else gain + 2 * (p - lag), asked=not back)

            def ask_high():
                dve.sem_inc(act_req, 1)
                REQ.n += 1

            def low_part(dst, kt, gain=None, asked=False):
                if not asked:
                    ask_high()
                dve.wait_ge(unit_done, W.U.at(1))
                b = W.bank()
                dve.wait_ge(act_done, W.R.next())
                hi, lo = XH[dst], XL[dst]
                if gain is None:
                    TT(lo[:, kt:kt + 2, :].rearrange("p k s -> p (k s)"), b,
                            hi[:, kt:kt + 2, :].rearrange("p k s -> p (k s)").bitcast(F32), ALU.subtract).then_inc(unit_free, 1)
                    dve.wait_ge(unit_free, W.U.next())
                else:
                    for k in range(2):
                        ins = STT(lo[:, kt + k, :], b[:, k * S:(k + 1) * S], gcol[:, gain + k:gain + k + 1],
                                  hi[:, kt + k, :].bitcast(F32), ALU.mult, ALU.subtract)
                    ins.then_inc(unit_free, 1)
                    dve.wait_ge(unit_free, W.U.next())

            def norm_split(dst, kt0, kts, gain, x, w, back=(), scaled=False, meanwhile=None):
                if not scaled:
                    row_rstd(x, w)

                def fill(p, s):
                    if p == 2 and meanwhile:
                        meanwhile()
                    TS(s[:, 0, :], x[:, 0, p * 256:(p + 1) * 256], sm[:, 2:3], None, ALU.mult)
                    TS(s[:, 1, :], x[:, 1, p * 256:(p + 1) * 256], sm[:, 3:4], None, ALU.mult).then_inc(unit_src, 1)
                    dve.wait_ge(unit_src, SRC.next())
                turn_and_split(dst, kt0, kts, gain, fill, back)

            def split_plain(dst, kt0, kts, x, back=()):
                def fill(p, s):
                    v = cols(x, p // 2)[:, :, (p % 2) * 256:(p % 2 + 1) * 256]
                    CP(s, v).then_inc(unit_src, 1)
                    dve.wait_ge(unit_src, SRC.next())
                turn_and_split(dst, kt0, kts, None, fill, back)

            def product_and_turn(dst, total, side):
                for k in range(5):
                    if k < 4:
                        take_add_times(cols(total, k), cols(side, k))
                        for p in range(2):
                            v = cols(total, k)[:, :, p * 256:(p + 1) * 256]
                            slot = W.U.slot(4, p if k == 0 else 2 + p)
                            CP(stage[:, slot, :].rearrange("p (t n) -> p t n", t=T), v).then_inc(unit_src, 1)
                            dve.wait_ge(unit_src, SRC.next())
                            ask_high()
                    if k:
                        low_part(dst, 4 * k - 4, asked=True)
                        low_part(dst, 4 * k - 2, asked=True)
                activations()

            def activations():
                tell(x_split)

            def sigmoid(w=CW):
                e = etmp[:, :, 0:w]
                TS(e, e, 1.0, None, ALU.add).then_inc(step, 1)
                dve.wait_ge(step, V.next())
                dve.reciprocal(e, e).then_inc(step, 1)
                dve.wait_ge(step, V.next())

            def ask_exp(c):
                dve.wait_ge(w_used, W.E.next(c.grans))
                a = acc[W.C.slot(2)]
                W.C.next()
                dve.sem_inc(act_req, 1)
                REQ.n += 1
                dve.wait_ge(act_done, W.R.next())
                return a

            def take_copy(dst, w=CW):
                W.split_next()
                dve.wait_ge(w_used, W.E.next(this().grans))
                a = acc[W.C.slot(2)]
                W.C.next()
                CP(dst, a[:, :, 0:w]).then_inc(acc_free, 1)
                dve.wait_ge(acc_free, W.C.at(0))

            def take_sigmoid(dst):
                W.split_next()
                a = ask_exp(this())
                TS(etmp[:], etmp[:], 1.0, None, ALU.add).then_inc(step, 1)
                dve.wait_ge(step, V.next())
                dve.reciprocal(dst, etmp[:]).then_inc(acc_free, 1)
                dve.wait_ge(acc_free, W.C.at(0))
                W.more()

            def take_silu(dst, c=None):
                if c is None:
                    W.split_next()
                    c = this()
                a = ask_exp(c)
                sigmoid()
                W.more()
                TT(dst, a[:], etmp[:], ALU.mult).then_inc(acc_free, 1)
                dve.wait_ge(acc_free, W.C.at(0))

            def take_times(dst):
                W.split_next()
                dve.wait_ge(w_used, W.E.next(this().grans))
                a = acc[W.C.slot(2)]
                W.C.next()
                TT(dst, a[:], dst, ALU.mult).then_inc(acc_free, 1)
                dve.wait_ge(acc_free, W.C.at(0))

            def take_add_times(dst, side):
                W.split_next()
                dve.wait_ge(w_used, W.E.next(this().grans))
                a = acc[W.C.slot(2)]
                W.C.next()
                TT(side, a[:], side, ALU.mult).then_inc(acc_free, 1)
                dve.wait_ge(acc_free, W.C.at(0))
                TT(dst, dst, side, ALU.add).then_inc(step, 1)
                dve.wait_ge(step, V.next())

            def take_add(dst):
                W.split_next()
                dve.wait_ge(w_used, W.E.next(this().grans))
                a = acc[W.C.slot(2)]
                W.C.next()
                TT(dst, a[:], dst, ALU.add).then_inc(acc_free, 1)
                dve.wait_ge(acc_free, W.C.at(0))

            def take(c):
                into = places.pop(0)
                dve.wait_ge(w_used, W.E.next(c.grans))
                a = acc[W.C.slot(2)]
                W.C.next()
                if c.name in GATED:
                    dve.sem_inc(act_req, 1)
                    REQ.n += 1
                    dve.wait_ge(act_done, W.R.next())
                    if GATED[c.name] == "silu":
                        CP(into, a[:]).then_inc(acc_free, 1)
                        dve.wait_ge(acc_free, W.C.at(0))
                    else:
                        dve.sem_inc(acc_free, 1)
                    TS(etmp[:], etmp[:], 1.0, None, ALU.add).then_inc(step, 1)
                    dve.wait_ge(step, V.next())
                    if GATED[c.name] == "silu":
                        dve.reciprocal(etmp[:], etmp[:]).then_inc(step, 1)
                        dve.wait_ge(step, V.next())
                        TT(into, into, etmp[:], ALU.mult).then_inc(step, 1)
                        dve.wait_ge(step, V.next())
                    else:
                        dve.reciprocal(into, etmp[:]).then_inc(step, 1)
                        dve.wait_ge(step, V.next())
                    return
                elif c.name == "conv_out":
                    side, total = into
                    TT(side, a[:], side, ALU.mult).then_inc(acc_free, 1)
                    dve.wait_ge(acc_free, W.C.at(0))
                    TT(total, total, side, ALU.add).then_inc(step, 1)
                    dve.wait_ge(step, V.next())
                    return
                elif c.name in TIMES:
                    TT(into, a[:], into, ALU.mult).then_inc(acc_free, 1)
                else:
                    CP(into, a[:, :, 0:c.w]).then_inc(acc_free, 1)
                dve.wait_ge(acc_free, W.C.at(0))
            W.take = take

            def cols(x, k):
                return x[:, k] if len(x.shape) == 4 else x[:, :, k * CW:(k + 1) * CW]

            dve.sem_inc(unit_src, 1)
            SRC.n += 1
            dve.wait_ge(unit_done, W.U.at(1))
            CP(gcol[:], W.bank()[:, 0:NG]).then_inc(unit_free, 1)
            dve.wait_ge(unit_free, W.U.next())
            dve.wait_ge(x_in, 16)
            W.split_next()
            norm_split("A", 0, KT, GCOL["norm_mix_g"], xres[:], D)
            activations()
            dve.wait_ge(small_in, 5 * 16)
            dve.wait_ge(c_in, 16)
            TWO_PI = 6.283185307179586
            c1 = 6.28125
            c2 = 2029 / 2 ** 20
            c3 = TWO_PI - c1 - c2
            posf, ang, turns, tmp = sm[:, 0:2], work[:, 0:64], work[:, 64:128], work[:, 128:192]
            CP(posf, posi[:]).then_inc(step, 1)
            dve.wait_ge(step, V.next())
            for t in range(T):
                TS(ang[:, t * 32:(t + 1) * 32], con("inv_freq"), posf[:, t:t + 1], None, ALU.mult).then_inc(step, 1)
                dve.wait_ge(step, V.next())
            csv = cs[:]
            for k, (shift, add) in enumerate(((0.0, 0.0), (0.25, TWO_PI / 4))):
                TS(turns, ang, 1.0 / TWO_PI, shift, ALU.mult, ALU.add).then_inc(step, 1)
                dve.wait_ge(step, V.next())
                TS(turns, turns, 12582912.0, -12582912.0, ALU.add, ALU.add).then_inc(step, 1)
                dve.wait_ge(step, V.next())
                STT(tmp, turns, -c1, ang, ALU.mult, ALU.add).then_inc(step, 1)
                dve.wait_ge(step, V.next())
                STT(tmp, turns, -c2, tmp, ALU.mult, ALU.add).then_inc(step, 1)
                dve.wait_ge(step, V.next())
                STT(tmp, turns, -c3, tmp, ALU.mult, ALU.add).then_inc(step, 1)
                dve.wait_ge(step, V.next())
                TS(tmp, tmp, add, 3.1415925, ALU.add, ALU.min).then_inc(step, 1)
                dve.wait_ge(step, V.next())
                ins = TS(csv[:, :, k, :], tmp.rearrange("p (t n) -> p t n", t=T), -3.1415925, None, ALU.max)
                if k == 0:
                    ins.then_inc(step, 1)
                    dve.wait_ge(step, V.next())
            ins.then_inc(act_req, 1)
            dve.wait_ge(act_req, REQ.next())
            dve.wait_ge(act_done, W.R.next())
            dve.sem_inc(unit_src, 1)
            SRC.n += 1

            def take_queries():
                dve.wait_ge(w_used, W.E.next(this().grans))
                a = acc[W.C.slot(2)]
                W.C.next()
                return a

            def turn_queries(j):
                for t in range(T):
                    for half in range(2):
                        dve.wait_ge(unit_done, W.U.at(1))
                        p0 = 4 * j + 2 * half
                        TS(qaT[:, p0:p0 + 2, t * P:(t + 1) * P], W.bank()[:, 0:256].rearrange("p (h s) -> p h s", h=2),
                           float(AD) ** -0.5, None, ALU.mult).then_inc(unit_free, 1)
                        dve.wait_ge(unit_free, W.U.next())

            for j in range(2):
                W.split_next()
                if j == 1:
                    turn_queries(0)
                a = take_queries()
                first = 1 - j
                for t in range(T):
                    for half in range(2):
                        slot = W.U.slot(4, first + 2 * t + half)
                        if first and t == 1 and half == 1:
                            dve.wait_ge(b_in, 16 * 3)
                            dve.wait_ge(unit_done, W.U.at(1))
                            TT(bias_row, W.bank()[0:AH, 0:BIASW], bmask, ALU.add).then_inc(unit_free, 1)
                            dve.wait_ge(unit_free, W.U.next())
                            tell(b_row)
                        ins = CP(stage[:, slot, 0:256], a[:, t, half * 256:(half + 1) * 256])
                        if t == 1 and half == 1:
                            ins.then_inc(acc_free, 1)
                            dve.wait_ge(acc_free, W.C.at(0))
                            dve.sem_inc(unit_src, 1)
                            SRC.n += 1
                        else:
                            ins.then_inc(unit_src, 1)
                            dve.wait_ge(unit_src, SRC.next())
            W.split_next()
            turn_queries(1)
            W.background(7)
            dve.wait_ge(w_used, W.E.next(this().grans))
            a = acc[W.C.slot(2)]
            W.C.next()
            for t in range(T):
                u = stage[:, W.U.slot(4, t), :].rearrange("p (h d n) -> p h d n", h=AKV, d=2)
                k4 = a[:, t, 0:256].rearrange("p (h n) -> p h n", h=AKV)
                CP(u[:, :, 0, :], k4)
                CP(u[:, :, 1, :], k4).then_inc(unit_src, 1)
                dve.wait_ge(unit_src, SRC.next())
            CP(va, a[:, :, 256:512]).then_inc(acc_free, 1)
            dve.wait_ge(acc_free, W.C.at(0))
            W.back(3)
            for t in range(T):
                dve.wait_ge(unit_done, W.U.at(1))
                CP(kaT[:, :, t * P:(t + 1) * P], W.bank().rearrange("p (h s) -> p h s", h=AKV)).then_inc(unit_free, 1)
                dve.wait_ge(unit_free, W.U.next())
            places = [qb, kb, vb[:, :, 0:CW], vb[:, :, CW:2 * CW], sm[:, 64:96].rearrange("p (t n) -> p t n", t=T),
                      ob[:, :, 0:CW], ob[:, :, CW:2 * CW]]
            dve.wait_ge(b_ready, 32)
            for g in range(AKV):
                for b in range(T):
                    nk = (b + 1) * P
                    dve.sem_inc(unit_src, 1)
                    SRC.n += 1
                    dve.sem_inc(unit_src, 1)
                    SRC.n += 1
                    W.back(SWA_BACK[g * T + b][0])
                    for u in range(2):
                        dve.wait_ge(unit_done, W.U.at(1))
                        bt = bias_t[:, AG * g:AG * (g + 1), 256 - nk:256].rearrange("p (a b) k -> p b a k", b=2)[:, u]
                        TT(work[:, u * 2 * nk:(u + 1) * 2 * nk].rearrange("p (h k) -> p h k", h=2),
                                W.bank()[:, 0:2 * nk].rearrange("p (h k) -> p h k", h=2), bt, ALU.add).then_inc(unit_free, 1)
                        dve.wait_ge(unit_free, W.U.next())
                    sc = work[:, 0:4 * nk].rearrange("p (h k) -> p h k", h=4)
                    dve.tensor_reduce(sm[:, 16:20], sc, AX.X, ALU.max).then_inc(step, 1)
                    dve.wait_ge(step, V.next())
                    four = "p (b a) -> p b a"
                    sk = sinks[:, AG * g:AG * g + 4].rearrange("p (a b) -> p b a", b=2)
                    m4, e4 = sm[:, 16:20].rearrange(four, b=2), sm[:, 28:32].rearrange(four, b=2)
                    TT(m4, m4, sk, ALU.max).then_inc(step, 1)
                    dve.wait_ge(step, V.next())
                    TT(e4, sk, m4, ALU.subtract).then_inc(step, 1)
                    dve.wait_ge(step, V.next())
                    TS(sm[:, 16:20], sm[:, 16:20], -1.0, None, ALU.mult).then_inc(step, 1)
                    dve.wait_ge(step, V.next())
                    for _ in range(5):
                        dve.sem_inc(act_req, 1)
                        REQ.n += 1
                    for _ in range(5):
                        dve.wait_ge(act_done, W.R.next())
                    for u in range(b + 1):
                        dve.sem_inc(unit_src, 1)
                        SRC.n += 1
                    TT(sm[:, 24:28], sm[:, 24:28], sm[:, 32:36], ALU.add).then_inc(step, 1)
                    dve.wait_ge(step, V.next())
                    dve.reciprocal(sm[:, 24:28], sm[:, 24:28]).then_inc(step, 1)
                    dve.wait_ge(step, V.next())
                    W.back(SWA_BACK[g * T + b][1])
                    for u in range(b + 1):
                        dve.wait_ge(unit_done, W.U.at(1))
                        CP(work[:, 1024 + u * 512:1024 + (u + 1) * 512], W.bank()).then_inc(unit_free, 1)
                        dve.wait_ge(unit_free, W.U.next())
                    dve.sem_inc(unit_src, 1)
                    SRC.n += 1
                    W.back(SWA_BACK[g * T + b][2])
                    dve.wait_ge(unit_done, W.U.at(1))
                    y = stage[:, W.U.slot(4, 1 if b == T - 1 else 6), b * 256:(b + 1) * 256]
                    scale = sm[:, 24:28].rearrange("p (b a) -> p a b", b=2).unsqueeze(3).to_broadcast([P, 2, 2, AD])
                    TT(y.rearrange("p (a b n) -> p a b n", a=2, b=2), W.bank()[:, 0:256].rearrange("p (a b n) -> p a b n", a=2, b=2),
                       scale, ALU.mult).then_inc(unit_free, 1)
                    dve.wait_ge(unit_free, W.U.next())
                dve.sem_inc(unit_src, 1)
                SRC.n += 1
                low_part("B", 2 * g)
            activations()
            W.back_end()
            dve.sem_inc(act_req, 1)
            REQ.n += 1
            dve.memset(att[:], 0.0).then_inc(step, 1)
            dve.wait_ge(step, V.next())
            dve.memset(glT[0:32, :], 1.0).then_inc(step, 1)
            dve.wait_ge(step, V.next())
            dve.wait_ge(act_done, W.R.next())
            CP(W.slot()[:, 0:32], sm[:, 64:96]).then_inc(unit_src, 1)
            dve.wait_ge(unit_src, SRC.next())
            W.background(6)
            places += [cols(merged1, k) for k in (0, 1, 2, 0, 1, 2)]
            W.back(2)
            dve.wait_ge(unit_done, W.U.at(1))
            CP(glT[0:RANK, :], W.bank()[0:RANK, 0:256]).then_inc(unit_free, 1)
            dve.wait_ge(unit_free, W.U.next())
            dve.sem_inc(unit_src, 1)
            SRC.n += 1
            dve.sem_inc(unit_src, 1)
            SRC.n += 1
            W.back(3)
            dve.wait_ge(gla_in, 48)
            for t in range(T):
                dve.wait_ge(unit_done, W.U.at(1))
                z = W.bank()
                TS(loga[:, t, :], z, 0.0, None, ALU.min).then_inc(step, 1)
                dve.wait_ge(step, V.next())
                STT(gtmp[:, t, :], loga[:, t, :], -2.0, z, ALU.mult, ALU.add).then_inc(step, 1)
                dve.wait_ge(step, V.next())
                dve.sem_inc(act_req, 1)
                REQ.n += 1
                dve.wait_ge(act_done, W.R.next())
                TT(loga[:, t, :], loga[:, t, :], gtmp[:, t, :], ALU.subtract).then_inc(step, 1)
                dve.wait_ge(step, V.next())
                TS(loga[:, t, :], loga[:, t, :], 1.0 / TAU, None, ALU.mult).then_inc(unit_free, 1)
                dve.wait_ge(unit_free, W.U.next())
            for t in range(T):
                dve.sem_inc(unit_src, 1)
                SRC.n += 1
                dve.sem_inc(unit_src, 1)
                SRC.n += 1
                W.back(2)
                dve.wait_ge(unit_done, W.U.at(1))
                dve.sem_inc(act_req, 1)
                REQ.n += 1
                dve.wait_ge(act_done, W.R.next())
                STT(qb[:, t, :], qb[:, t, :], float(BK) ** -0.5, gtmp[:, 0, :], ALU.mult, ALU.mult).then_inc(unit_free, 1)
                dve.wait_ge(unit_free, W.U.next())
                kd_slot = stage[:, W.U.slot(4, 2), :]
                TT(kd_slot, kb[:, t, :], gtmp[:, 1, :], ALU.mult).then_inc(step, 1)
                dve.wait_ge(step, V.next())
                dve.wait_ge(unit_done, W.U.at(1))
                dve.sem_inc(act_req, 1)
                REQ.n += 1
                dve.wait_ge(act_done, W.R.next())
                TT(kb[:, t, :], kb[:, t, :], gtmp[:, 0, :], ALU.mult).then_inc(unit_free, 1)
                dve.wait_ge(unit_free, W.U.next())
                dve.sem_inc(unit_src, 1)
                SRC.n += 1
                dve.sem_inc(unit_src, 1)
                SRC.n += 1
                W.back(1)
                for dst in (qdT, kdT):
                    dve.wait_ge(unit_done, W.U.at(1))
                    CP(dst[:, :, t * P:(t + 1) * P], W.bank().rearrange("p (h s) -> p h s", h=BH)).then_inc(unit_free, 1)
                    dve.wait_ge(unit_free, W.U.next())
            dve.sem_inc(unit_src, 1)
            SRC.n += 1
            W.back(1)
            dve.wait_ge(unit_done, W.U.at(1))
            dve.sem_inc(act_req, 1)
            REQ.n += 1
            dve.wait_ge(act_done, W.R.next())
            dve.memset(sm[:, 40:41], 0.0).then_inc(unit_free, 1)
            dve.wait_ge(unit_free, W.U.next())
            for h in range(BH):
                dve.sem_inc(unit_src, 1)
                SRC.n += 1
                dve.sem_inc(unit_src, 1)
                SRC.n += 1
                W.back(2)
                for t in range(T):
                    dve.wait_ge(unit_done, W.U.at(1))
                    dve.copy_predicated(att[:, t, :], con("causal").bitcast(I32), W.bank()[:, 0:P]).then_inc(unit_free, 1)
                    dve.wait_ge(unit_free, W.U.next())

                def new_state(n, h=h):
                    dve.sem_inc(unit_src, 1)
                    SRC.n += 1
                    dve.wait_ge(unit_done, W.U.at(1))
                    if n == 0:
                        CP(state[:, 1, :], W.bank()[:, 0:BV]).then_inc(unit_free, 1)
                        dve.wait_ge(unit_free, W.U.next())
                    else:
                        STT(state[:, (n + 1) % 2, :], state[:, n % 2, :], dec[:, h * 4 + n:h * 4 + n + 1],
                                 W.bank()[:, 0:BV], ALU.mult, ALU.add).then_inc(unit_free, 1)
                        dve.wait_ge(unit_free, W.U.next())

                def take_out(t, h=h):
                    dve.sem_inc(unit_src, 1)
                    SRC.n += 1
                    W.back(1 if t == 0 else 3)
                    dve.wait_ge(unit_done, W.U.at(1))
                    CP(og[:, t, :], W.bank()[:, 0:BV]).then_inc(unit_free, 1)
                    dve.wait_ge(unit_free, W.U.next())
                    ttr(etmp[:, 0, 0:BV], og[:, t, :], og[:, t, :], sm[:, t:t + 1]).then_inc(step, 1)
                    dve.wait_ge(step, V.next())
                new_state(0)
                take_out(0)
                new_state(1)
                new_state(2)
                take_out(1)
                rsqrt(2, BV)
                for t in range(T):
                    STT(og[:, t, :], og[:, t, :], sm[:, 2 + t:3 + t], gla_g, ALU.mult, ALU.mult).then_inc(step, 1)
                    dve.wait_ge(step, V.next())
                TT(W.slot().rearrange("p (t n) -> p t n", t=T), og, ob[:, :, h * BV:(h + 1) * BV], ALU.mult).then_inc(unit_src, 1)
                dve.wait_ge(unit_src, SRC.next())
                low_part("B", 8 + 2 * h)
            activations()
            W.back_end()
            take_sigmoid(cols(merged1, 3))
            take_times(cols(merged1, 3))
            for k in range(4):
                take_sigmoid(cols(side1, k))
            product_and_turn("A", merged1, side1)
            for k in range(4):
                take_add(cols(xres, k))
                row_part(xres, k)
            row_end()
            norm_split("B", 0, KT, GCOL["norm_ffn_g"], xres[:], D, scaled=True)
            activations()

            hid = work[:, 0:1024].rearrange("p (t n) -> p t n", t=T)
            gate_c, up_c = next(cc for nm, _, cc in SEG if nm == "ffn_up")

            def take_hidden(i):
                for p in range(2):
                    dve.wait_ge(unit_done, W.U.at(1))
                    CP(ffT[:, bass.ds(i * 4 + 2 * p, 2), :], W.bank().rearrange("p (k s) -> p k s", k=2)).then_inc(unit_free, 1)
                    dve.wait_ge(unit_free, W.U.next())

            def ffn_pass(i, first=False):
                W.split_next()
                take_silu(hid, gate_c)
                if not first:
                    take_hidden(i - 1)
                W.split_next()
                dve.wait_ge(w_used, W.E.next(up_c.grans))
                a = acc[W.C.slot(2)]
                W.C.next()
                TT(hid, a[:], hid, ALU.mult).then_inc(acc_free, 1)
                dve.wait_ge(acc_free, W.C.at(0))
                for p in range(2):
                    CP(stage[:, W.U.slot(4, p), :].rearrange("p (t n) -> p t n", t=T), hid[:, :, p * 256:(p + 1) * 256]).then_inc(unit_src, 1)
                    dve.wait_ge(unit_src, SRC.next())
            n = FF // CW
            ffn_pass(0, True)
            with engine_loop(dve, (n - 3) // 2, {W.G: 32, W.E: 32, W.C: 4, W.U: 4, W.R: 2, V: 4, SRC: 4, REQ: 2}) as i:
                ffn_pass(i * 2 + 1)
                ffn_pass(i * 2 + 2)
            W.next += 2 * (n - 5)
            ffn_pass(n - 2)
            ffn_pass(n - 1)
            take_hidden(n - 1)

            def down_pass(q, i, lagged):
                if lagged:
                    dve.wait_ge(w_used, W.G.at(-8))
                dve.sem_inc(act_req, 1)
                REQ.n += 1
                dve.wait_ge(act_done, W.R.next())
                for k in range(4):
                    ins = TT(XL["A"][:, 4 * q + k, :], ffT[:, bass.ds(i + k, 1), :].rearrange("p a s -> p (a s)"),
                             XH["A"][:, 4 * q + k, :].bitcast(F32), ALU.subtract)
                ins.then_inc(step, 1)
                dve.wait_ge(step, V.next())
                XS.n += 1
                tell(x_split)
                for _ in range(8):
                    split(GRAN)
            down_pass(0, 0, False)
            down_pass(1, 4, False)
            with engine_loop(dve, (FT // 4 - 3) // 2, {W.G: 16, W.R: 2, V: 2, REQ: 2, XS: 2}) as i:
                down_pass(0, i * 8 + 8, True)
                down_pass(1, i * 8 + 12, True)
            down_pass(0, FT - 4, True)
            W.next += FT // 4 - 1
            W.E.n += 2 * FT
            dve.wait_ge(mem_in, 16)
            row_rstd(memx, D)
            W.split_next()
            dve.wait_ge(w_used, W.E.at(0))

            def add_sums(tiles):
                for t in tiles:
                    sums = (acc[0][:], acc[1][:], bankt[:, 0:2, :], bankt[:, 2:4, :])[t]
                    x = xres[:, t // 2, (t % 2) * 1024:(t % 2 + 1) * 1024].rearrange("p (a n) -> p a n", a=2)
                    ins = TT(x, sums, x, ALU.add)
                ins.then_inc(step, 1)
                dve.wait_ge(step, V.next())
            add_sums((2, 3))
            norm_split("B", 0, KT, GCOL["mem_norm_g_2"], memx, D, scaled=True, meanwhile=lambda: add_sums((0, 1)))
            activations()

            def head_norms(x, n, dim, w):
                for t in range(T):
                    for h in range(n):
                        v = x[:, t, h * w:h * w + dim]
                        ins = ttr(etmp[:, t, h * dim:(h + 1) * dim], v, v, sm[:, t * n + h:t * n + h + 1])
                ins.then_inc(step, 1)
                dve.wait_ge(step, V.next())

            def turn_keys(j):
                for hh in range(2):
                    dve.wait_ge(unit_done, W.U.at(1))
                    b = W.bank()
                    for k in range(2):
                        g = GCOL["mem_kn_g_2"] + k
                        ins = TS(memkT[:, 2 * j + hh, k, :], b[:, k * S:(k + 1) * S], gcol[:, g:g + 1], None, ALU.mult)
                    ins.then_inc(unit_free, 1)
                    dve.wait_ge(unit_free, W.U.next())

            kx = work[:, 0:1024].rearrange("p (t n) -> p t n", t=T)

            def take_keys():
                dve.wait_ge(w_used, W.E.next(this().grans))
                a = acc[W.C.slot(2)]
                W.C.next()
                CP(kx, a[:]).then_inc(acc_free, 1)
                dve.wait_ge(acc_free, W.C.at(0))

            def stage_keys():
                head_norms(kx, 2, ED, ED)
                rsqrt(4, ED)
                for hh in range(2):
                    s = stage[:, W.U.slot(4, hh), :].rearrange("p (t n) -> p t n", t=T)
                    TS(s[:, 0, :], kx[:, 0, hh * ED:(hh + 1) * ED], sm[:, 4 + hh:5 + hh], None, ALU.mult)
                    TS(s[:, 1, :], kx[:, 1, hh * ED:(hh + 1) * ED], sm[:, 6 + hh:7 + hh], None, ALU.mult).then_inc(unit_src, 1)
                    dve.wait_ge(unit_src, SRC.next())

            W.split_next()
            row_rstd(xres[:], D)
            dve.wait_ge(fin_in, 16)
            for t in range(T):
                ins = STT(xres[:, t, :], xres[:, t, :], sm[:, 2 + t:3 + t], fin_g, ALU.mult, ALU.mult)
            ins.then_inc(step, 1)
            dve.wait_ge(step, V.next())
            take_keys()
            W.split_next()
            stage_keys()
            row_rstd(xres[:], D)
            CP(sm[:, 110:112], sm[:, 2:4]).then_inc(step, 1)
            dve.wait_ge(step, V.next())
            take_keys()
            turn_keys(0)
            stage_keys()
            W.background(2)
            places += [cols(memv, 0), cols(memv, 1)]
            W.back(3)
            turn_keys(1)
            CP(sm[:, 2:4], sm[:, 110:112]).then_inc(step, 1)
            dve.wait_ge(step, V.next())
            norm_split("A", 0, KT, GCOL["norm_g_2"], xres[:], D, MEM_BACK, scaled=True)
            activations()
            W.back_end()
            places += [cols(merged2, k) for k in range(4)]
            for h2 in range(2):
                take_silu(ezs)
                W.split_next()
                dve.wait_ge(w_used, W.E.next(this().grans))
                a = acc[W.C.slot(2)]
                W.C.next()
                qx = area(0, 4).rearrange("p (t n) -> p t n", t=T)
                CP(qx, a[:]).then_inc(acc_free, 1)
                dve.wait_ge(acc_free, W.C.at(0))
                head_norms(qx, 2, ED, ED)
                W.background(2)
                W.back(2)
                rsqrt(4, ED)
                for t in range(T):
                    for hh in range(2):
                        TS(qx[:, t, hh * ED:(hh + 1) * ED], qx[:, t, hh * ED:(hh + 1) * ED], sm[:, 4 + 2 * t + hh:5 + 2 * t + hh], None, ALU.mult).then_inc(step, 1)
                        dve.wait_ge(step, V.next())
                for hh in range(2):
                    CP(W.slot().rearrange("p (t n) -> p t n", t=T), qx[:, :, hh * ED:(hh + 1) * ED]).then_inc(unit_src, 1)
                    dve.wait_ge(unit_src, SRC.next())
                    W.back(2)
                    dve.wait_ge(unit_done, W.U.at(1))
                    b = W.bank()
                    for k in range(2):
                        ins = TS(eqT[:, k, :], b[:, k * S:(k + 1) * S], gcol[:, GCOL["mem_qn_g_2"] + k:GCOL["mem_qn_g_2"] + k + 1], None, ALU.mult)
                    ins.then_inc(unit_free, 1)
                    dve.wait_ge(unit_free, W.U.next())
                    dve.sem_inc(unit_src, 1)
                    SRC.n += 1
                    W.back(2)
                    dve.wait_ge(unit_done, W.U.at(1))
                    TS(work[:, 0:512], W.bank(), float(ED) ** -0.5, None, ALU.mult).then_inc(unit_free, 1)
                    dve.wait_ge(unit_free, W.U.next())
                    dve.tensor_reduce(sm[:, 16:18], work[:, 0:512].rearrange("p (t k) -> p t k", t=T), AX.X, ALU.max, negate=True).then_inc(step, 1)
                    dve.wait_ge(step, V.next())
                    dve.sem_inc(act_req, 1)
                    REQ.n += 1
                    dve.sem_inc(act_req, 1)
                    REQ.n += 1
                    dve.wait_ge(act_done, W.R.next())
                    dve.wait_ge(act_done, W.R.next())
                    dve.sem_inc(unit_src, 1)
                    SRC.n += 1
                    W.back(1)
                    dve.reciprocal(sm[:, 24:26], sm[:, 24:26]).then_inc(step, 1)
                    dve.wait_ge(step, V.next())
                    dve.wait_ge(unit_done, W.U.at(1))
                    CP(work[:, 1024:1536], W.bank()).then_inc(unit_free, 1)
                    dve.wait_ge(unit_free, W.U.next())
                    dve.sem_inc(unit_src, 1)
                    SRC.n += 1
                    W.back(1)
                    dve.wait_ge(unit_done, W.U.at(1))
                    b = W.bank()
                    ns = stage[:, W.U.slot(4, 1), :].rearrange("p (t n) -> p t n", t=T)
                    for t in range(T):
                        ins = STT(ns[:, t, :], b[:, t * 256:(t + 1) * 256], sm[:, 24 + t:25 + t], ezs[:, t, hh * ED:(hh + 1) * ED],
                                  ALU.mult, ALU.mult)
                    ins.then_inc(unit_free, 1)
                    dve.wait_ge(unit_free, W.U.next())
                    dve.sem_inc(unit_src, 1)
                    SRC.n += 1
                    W.back(1)
                    low_part("B", 8 + 4 * h2 + 2 * hh)
                W.back_end()
            activations()
            for k in range(4):
                take_times(cols(merged2, k))
            def conv_split(h):
                for p in range(2):
                    y = cvT[:, p * 512:(p + 1) * 512]
                    dve.wait_ge(unit_done, W.U.at(1))
                    TT(y, W.bank(), y, ALU.mult).then_inc(act_req, 1)
                    dve.wait_ge(act_req, REQ.next())
                    dve.wait_ge(act_done, W.R.next())
                    kt = 4 * h + 2 * p
                    TT(XL["B"][:, kt:kt + 2, :].rearrange("p k s -> p (k s)"), y,
                       XH["B"][:, kt:kt + 2, :].rearrange("p k s -> p (k s)").bitcast(F32), ALU.subtract).then_inc(unit_free, 1)
                    dve.wait_ge(unit_free, W.U.next())

            def stage_pair(x):
                for p in range(2):
                    CP(stage[:, W.U.slot(4, p), :].rearrange("p (t n) -> p t n", t=T), x[:, :, p * 256:(p + 1) * 256]).then_inc(unit_src, 1)
                    dve.wait_ge(unit_src, SRC.next())

            dve.memset(vT[:, :, 0:2], 0.0).then_inc(step, 1)
            dve.wait_ge(step, V.next())
            for h in range(2):
                take_copy(cgt)
                if h == 1:
                    conv_split(0)
                W.split_next()
                dve.wait_ge(w_used, W.E.next(this().grans))
                a = acc[W.C.slot(2)]
                W.C.next()
                TT(cgt, a[:], cgt, ALU.mult).then_inc(acc_free, 1)
                dve.wait_ge(acc_free, W.C.at(0))
                stage_pair(cgt)
                take_copy(bgt)
                for p in range(2):
                    dve.wait_ge(unit_done, W.U.at(1))
                    CP(vT[:, 2 * p:2 * p + 2, 2:S + 2], W.bank().rearrange("p (k s) -> p k s", k=2)).then_inc(unit_free, 1)
                    dve.wait_ge(unit_free, W.U.next())
                for j in range(CONVK):
                    for kt in range(4):
                        g = GCOL["conv_w_2"] + 8 * j + 4 * h + kt
                        y, v = cvT[:, kt * S:(kt + 1) * S], vT[:, kt, j:S + j]
                        if j == 0:
                            ins = TS(y, v, gcol[:, g:g + 1], None, ALU.mult)
                        else:
                            ins = STT(y, v, gcol[:, g:g + 1], y, ALU.mult, ALU.add)
                    ins.then_inc(step, 1)
                    dve.wait_ge(step, V.next())
                W.split_next()
                a = ask_exp(this())
                sigmoid()
                W.more()
                TT(etmp[:], a[:], etmp[:], ALU.mult).then_inc(acc_free, 1)
                dve.wait_ge(acc_free, W.C.at(0))
                TT(bgt, bgt, etmp[:], ALU.mult).then_inc(step, 1)
                dve.wait_ge(step, V.next())
                stage_pair(bgt)
            def stage_normed(x):
                row_rstd(x, LORA)
                for p in range(2):
                    s = stage[:, W.U.slot(4, p), :].rearrange("p (t n) -> p t n", t=T)
                    for t in range(T):
                        ins = TS(s[:, t, :], x[:, t, p * 256:(p + 1) * 256], sm[:, 2 + t:3 + t], None, ALU.mult)
                    ins.then_inc(unit_src, 1)
                    dve.wait_ge(unit_src, SRC.next())
            take_copy(cgt)
            conv_split(1)
            stage_normed(cgt)
            take_copy(bgt)
            for p in range(2):
                low_part("B", 8 + 2 * p, GCOL["mla_q_norm_g_2"] + 2 * p)
            stage_normed(bgt)

            def rotate(dst, x, n):
                r = rot[:, :, 0:n, :]
                for t in range(T):
                    a, b, si, co = x[:, t, :, 0:32], x[:, t, :, 32:64], csb(t, 0, n), csb(t, 1, n)
                    TT(dst[:, t, :, 0:32], a, co, ALU.mult)
                    TT(r[:, 2 * t], b, si, ALU.mult)
                    TT(dst[:, t, :, 32:64], b, co, ALU.mult)
                    ins = TT(r[:, 2 * t + 1], a, si, ALU.mult)
                ins.then_inc(step, 1)
                dve.wait_ge(step, V.next())
                for t in range(T):
                    TT(dst[:, t, :, 0:32], dst[:, t, :, 0:32], r[:, 2 * t], ALU.subtract)
                    ins = TT(dst[:, t, :, 32:64], dst[:, t, :, 32:64], r[:, 2 * t + 1], ALU.add)
                ins.then_inc(step, 1)
                dve.wait_ge(step, V.next())

            def csb(t, k, n):
                v = cs[:, t, k, :]
                return v.unsqueeze(1).to_broadcast([P, n, 32]) if n > 1 else v.unsqueeze(1)

            dve.wait_ge(w_used, W.E.next(1))
            a = acc[W.C.slot(2)]
            W.C.next()
            kr = work[:, 0:128].rearrange("p (t n) -> p t n", t=T)
            CP(kr, a[:, :, 0:DR]).then_inc(acc_free, 1)
            dve.wait_ge(acc_free, W.C.at(0))
            for p in range(2):
                low_part("B", 12 + 2 * p, GCOL["mla_kv_norm_g_2"] + 2 * p)
            for t in range(T):
                ttr(etmp[:, 1, 0:DR], kr[:, t, :], kr[:, t, :], sm[:, t:t + 1]).then_inc(step, 1)
                dve.wait_ge(step, V.next())
            rsqrt(2, DR)
            for t in range(T):
                STT(kr[:, t, :], kr[:, t, :], sm[:, 2 + t:3 + t], rope_g[:, 1, :], ALU.mult, ALU.mult).then_inc(step, 1)
                dve.wait_ge(step, V.next())
            twice = W.slot()[:, 0:256].rearrange("p (t h n) -> p t h n", t=T, h=2)
            rotate(twice[:, :, 0:1, :], kr.unsqueeze(2), 1)
            CP(twice[:, :, 1, :], twice[:, :, 0, :]).then_inc(unit_src, 1)
            dve.wait_ge(unit_src, SRC.next())
            dve.wait_ge(unit_done, W.U.at(1))
            CP(krT, W.bank()[:, 0:S]).then_inc(unit_free, 1)
            dve.wait_ge(unit_free, W.U.next())
            activations()
            mla_cc = next(cc for nm, _, cc in SEG if nm == "mla")

            def mla_pair(i, pr, uq, ukv, *others):
                ks = MLA_BACK[pr % 2]
                if pr == 0:
                    W.ahead(4)
                dve.wait_ge(w_used, W.E.next(uq.grans))
                a = acc[W.C.slot(2)]
                W.C.next()
                CP(qs, a[:, :, 0:384]).then_inc(acc_free, 1)
                dve.wait_ge(acc_free, W.C.at(0))
                W.background(len(others), False, 2)
                dve.wait_ge(w_used, W.E.next(ukv.grans))
                a = acc[W.C.slot(2)]
                W.C.next()
                kv4 = a[:].rearrange("p t (h n) -> p t h n", h=2)
                CP(kvv.rearrange("p t (h n) -> p t h n", h=2), kv4[:, :, :, DN:256]).then_inc(step, 1)
                dve.wait_ge(step, V.next())
                kx = kx_mla.rearrange("p (t h n) -> p t h n", t=T, h=2)
                CP(kx, kv4[:, :, :, 0:DN]).then_inc(acc_free, 1)
                dve.wait_ge(acc_free, W.C.at(0))
                j = i * 2 + pr // 2
                gate = silz[:, bass.ds(j, 1), :, :].rearrange("p a t n -> p (a t) n")
                total = merged2[:, bass.ds(j, 1), :, :].rearrange("p a t n -> p (a t) n")
                places.extend([gate] if pr % 2 == 0 else [side2, (side2, total)])
                W.back(ks[0])
                for t in range(T):
                    for h in range(2):
                        for q, (x, n, o) in enumerate(((qs[:, t, h * 192:h * 192 + DN], DN, 0),
                                                       (qs[:, t, h * 192 + DN:(h + 1) * 192], DR, 4), (kx[:, t, h, :], DN, 8))):
                            k = 6 * t + 3 * h + q
                            ins = ttr(squares[:, k, 0:n], x, x, sm[:, o + 2 * t + h:o + 2 * t + h + 1])
                ins.then_inc(step, 1)
                dve.wait_ge(step, V.next())
                TS(sm[:, 4:8], sm[:, 4:8], float(DN) / DR, None, ALU.mult).then_inc(step, 1)
                dve.wait_ge(step, V.next())
                rsqrt(12, DN)
                s = W.slot().rearrange("p (t n) -> p t n", t=T)
                for t in range(T):
                    for h in range(2):
                        ins = TS(s[:, t, h * DN:(h + 1) * DN], qs[:, t, h * 192:h * 192 + DN], sm[:, 12 + 2 * t + h:13 + 2 * t + h], None, ALU.mult)
                ins.then_inc(unit_src, 1)
                dve.wait_ge(unit_src, SRC.next())
                s2 = stage[:, W.U.slot(4, 1), 0:256].rearrange("p (t h n) -> p t h n", t=T, h=2)
                rq = rop[:, 1:3, :].rearrange("p t (h n) -> p t h n", h=2)
                for t in range(T):
                    for h in range(2):
                        ins = STT(rq[:, t, h, :], qs[:, t, h * 192 + DN:(h + 1) * 192], sm[:, 16 + 2 * t + h:17 + 2 * t + h],
                                  rope_g[:, 0, :], ALU.mult, ALU.mult)
                ins.then_inc(step, 1)
                dve.wait_ge(step, V.next())
                rotate(s2, rq, 2)
                dve.sem_inc(unit_src, 1)
                SRC.n += 1
                s = stage[:, W.U.slot(4, 2), :].rearrange("p (t n) -> p t n", t=T)
                for t in range(T):
                    for h in range(2):
                        ins = TS(s[:, t, h * DN:(h + 1) * DN], kx[:, t, h, :], sm[:, 20 + 2 * t + h:21 + 2 * t + h], None, ALU.mult)
                ins.then_inc(unit_src, 1)
                dve.wait_ge(unit_src, SRC.next())
                W.back(ks[1])
                dve.wait_ge(unit_done, W.U.at(1))
                TS(qnT, W.bank().rearrange("p (h s) -> p h s", h=2), gcol[:, GCOL["mla_qn_nope_g_2"]:GCOL["mla_qn_nope_g_2"] + 1],
                   None, ALU.mult).then_inc(unit_free, 1)
                dve.wait_ge(unit_free, W.U.next())
                dve.wait_ge(unit_done, W.U.at(1))
                CP(qrT, W.bank()[:, 0:S]).then_inc(unit_free, 1)
                dve.wait_ge(unit_free, W.U.next())
                dve.wait_ge(unit_done, W.U.at(1))
                TS(knT, W.bank().rearrange("p (h s) -> p h s", h=2), gcol[:, GCOL["mla_kn_nope_g_2"]:GCOL["mla_kn_nope_g_2"] + 1],
                   None, ALU.mult).then_inc(unit_free, 1)
                dve.wait_ge(unit_free, W.U.next())
                dve.sem_inc(unit_src, 1)
                SRC.n += 1
                dve.sem_inc(unit_src, 1)
                SRC.n += 1
                W.back(ks[2])
                for h in range(2):
                    dve.wait_ge(unit_done, W.U.at(1))
                    b = W.bank()
                    o = h * 384
                    STT(work[:, o:o + P], b[:, 0:P], MLA_SCALE, con("mla_mask"), ALU.mult, ALU.add).then_inc(step, 1)
                    dve.wait_ge(step, V.next())
                    TS(work[:, o + P:o + 2 * P], b[:, P:2 * P], MLA_SCALE, None, ALU.mult).then_inc(step, 1)
                    dve.wait_ge(step, V.next())
                    STT(work[:, o + 2 * P:o + 3 * P], b[:, 2 * P:3 * P], MLA_SCALE, con("mla_mask"), ALU.mult, ALU.add).then_inc(unit_free, 1)
                    dve.wait_ge(unit_free, W.U.next())
                    dve.tensor_reduce(sm[:, 16 + 2 * h:17 + 2 * h], work[:, o:o + P], AX.X, ALU.max, negate=True).then_inc(step, 1)
                    dve.wait_ge(step, V.next())
                    dve.tensor_reduce(sm[:, 17 + 2 * h:18 + 2 * h], work[:, o + P:o + 3 * P], AX.X, ALU.max, negate=True).then_inc(step, 1)
                    dve.wait_ge(step, V.next())
                    dve.sem_inc(act_req, 1)
                    REQ.n += 1
                    dve.sem_inc(act_req, 1)
                    REQ.n += 1
                for _ in range(4):
                    dve.wait_ge(act_done, W.R.next())
                dve.sem_inc(unit_src, 1)
                SRC.n += 1
                dve.sem_inc(unit_src, 1)
                SRC.n += 1
                W.back(ks[3])
                dve.reciprocal(sm[:, 24:28], sm[:, 24:28]).then_inc(step, 1)
                dve.wait_ge(step, V.next())
                for h in range(2):
                    dve.wait_ge(unit_done, W.U.at(1))
                    CP(work[:, 1024 + h * 384:1024 + (h + 1) * 384], W.bank()[:, 0:384]).then_inc(unit_free, 1)
                    dve.wait_ge(unit_free, W.U.next())
                dve.sem_inc(unit_src, 1)
                SRC.n += 1
                if pr < 3:
                    W.ahead(4)
                W.back_end()
                dve.wait_ge(unit_done, W.U.at(1))
                b = W.bank()
                for t in range(T):
                    for h in range(2):
                        o = (pr % 2) * 256 + h * DV
                        z = silz[:, bass.ds(j, 1), t, o:o + DV].rearrange("p a n -> p (a n)")
                        ins = STT(z, b[:, t * 256 + h * DV:t * 256 + (h + 1) * DV], sm[:, 24 + 2 * h + t:25 + 2 * h + t], z, ALU.mult, ALU.mult)
                ins.then_inc(unit_free, 1)
                dve.wait_ge(unit_free, W.U.next())
            with engine_loop(dve, 2, {W.G: 56, W.E: 56, W.C: 14, W.U: 32, W.R: 24, V: 88, SRC: 32, REQ: 24}) as i:
                for k in range(2):
                    mla_pair(i, 2 * k, *mla_cc[7 * k:7 * k + 3])
                    mla_pair(i, 2 * k + 1, *mla_cc[7 * k + 3:7 * k + 7])
            W.next += 14
            W.split_next()
            W.background(3)
            places += [cols(side3, k) for k in range(3)]
            split_plain("B", 0, KT, silz, (3,) * (KT // 2))
            activations()
            W.back_end()
            take_sigmoid(cols(side3, 3))
            product_and_turn("A", merged2, side3)
            for k in range(4):
                take_add(cols(xres, k))
            tell(out_ready)
            tell(out_ready)


_FLAT = ("norm_mix_g", "sinks", "b_gate", "gla_norm_g", "norm_ffn_g", "norm_final_g", "norm_g_2", "conv_w_2",
         "mla_q_norm_g_2", "mla_kv_norm_g_2", "mla_qn_nope_g_2", "mla_qn_rope_g_2", "mla_kn_nope_g_2", "mla_kn_rope_g_2",
         "mem_norm_g_2", "mem_qn_g_2", "mem_kn_g_2", "positions_2")


def kernel(**inputs):
    import concourse.bacc as _bacc
    from concourse.bass_utils import run_bass_kernel_spmd as _run

    nc = _bacc.Bacc("TRN2", target_bir_lowering=False, num_devices=1, dynamic_dma_scratch_size=1024)
    arrays, ap = {}, {}
    given = {n: np.ascontiguousarray(a) for n, a in inputs.items()}
    for n, a in given.items():
        given[n] = a.reshape(-1) if n in _FLAT else a if a.ndim == 2 and n == "rel_bias" else a.reshape(a.shape[-2:])
    given.update(const=CONST, onehot=ONEHOT, bias_mask=BIAS_MASK)
    for n, a in given.items():
        arrays[f"in_{n}_dram"] = a
        ap[n] = nc.dram_tensor(f"in_{n}_dram", a.shape, mybir.dt.from_np(a.dtype), kind="ExternalInput").ap()
    out = nc.dram_tensor("out_0_dram", (S, D), F32, kind="ExternalOutput").ap()
    scratch = nc.dram_tensor("bias_rows", (AH, P * (BIASW + 1)), F32, kind="Internal").ap()
    build(nc, ap, out, scratch)
    r = _run(nc, [arrays], core_ids=[0])
    return r.results[0]["out_0_dram"].reshape(1, S, D)
```
